# Optimizing a Trainium2 kernel written in Bass

```python
import jax
import jax.numpy as jnp
from jax import lax
import numpy as np

D_MODEL = 1024
BATCH = 1
SEQ = 512
DEPTH = 1

CHUNK = 64
N_META = 16
LN_EPS = 1e-5
RMS_EPS = 1e-6

HG_HEADS = 8
HG_DK = 128
HG_DV = D_MODEL // HG_HEADS
HG_K_WIDTH = HG_HEADS * HG_DK
HG_V_WIDTH = HG_HEADS * HG_DV

LRU_WIDTH = D_MODEL
LRU_BLOCKS = 8
LRU_BLOCK = LRU_WIDTH // LRU_BLOCKS
CONV_W = 4
LRU_C = 8.0

SPLIT_SIZES = (HG_K_WIDTH, HG_K_WIDTH, HG_V_WIDTH, HG_V_WIDTH, LRU_WIDTH, LRU_WIDTH, D_MODEL, D_MODEL)
IN_COLS = 2 * HG_K_WIDTH + 2 * HG_V_WIDTH + 2 * LRU_WIDTH + 2 * D_MODEL

N_EXPERTS = 64
TOP_K = 6
D_EXPERT = 256
D_SHARED = 256
ROUTED_SCALE = 2.5
EXPERT_BLOCK = 128

DEEPNORM_ALPHA = (2.0 * DEPTH) ** 0.25
DEEPNORM_BETA = (8.0 * DEPTH) ** -0.25

kernel_name = 'hybrid_hgrn2_rglru_moe_block'

def layer_norm(x, g, b):
    xf = x.astype(jnp.float32)
    mu = jnp.mean(xf, axis=-1, keepdims=True)
    var = jnp.mean(jnp.square(xf - mu), axis=-1, keepdims=True)
    y = (xf - mu) * lax.rsqrt(var + LN_EPS) * g.astype(jnp.float32) + b.astype(jnp.float32)
    return y.astype(x.dtype)

def hgrn2_mixer(q, f_pre, v, g_out, lb, norm_g):
    B, L, _ = q.shape
    f32 = jnp.float32
    f = lb + (1.0 - lb) * jax.nn.sigmoid(f_pre.astype(f32))
    log_f = jnp.log(f)
    k = 1.0 - f
    qf = jax.nn.silu(q.astype(f32))
    vf = v.astype(f32)
    pad = (-L) % CHUNK
    n_chunks = (L + pad) // CHUNK

    def to_chunks(t, d):
        t = jnp.pad(t, ((0, 0), (pad, 0), (0, 0)))
        return t.reshape(B, n_chunks, CHUNK, HG_HEADS, d).transpose(1, 0, 3, 2, 4)

    causal = jnp.tril(jnp.ones((CHUNK, CHUNK), dtype=bool))[:, :, None]

    def chunk_step(S, inp):
        qc, kc, vc, lfc = inp
        b = jnp.cumsum(lfc, axis=2)
        diff = b[:, :, :, None, :] - b[:, :, None, :, :]
        decay = jnp.exp(jnp.where(causal, diff, -jnp.inf))
        scores = jnp.einsum('bhtk,bhsk,bhtsk->bhts', qc, kc, decay)
        o = (jnp.einsum('bhts,bhsv->bhtv', scores, vc)
             + jnp.einsum('bhtk,bhkv->bhtv', qc * jnp.exp(b), S))
        b_last = b[:, :, -1:, :]
        S = (jnp.exp(b_last[:, :, 0, :])[..., None] * S
             + jnp.einsum('bhsk,bhsv->bhkv', kc * jnp.exp(b_last - b), vc))
        return S, o

    S0 = jnp.zeros((B, HG_HEADS, HG_DK, HG_DV), f32)
    _, o = lax.scan(chunk_step, S0, (to_chunks(qf, HG_DK), to_chunks(k, HG_DK),
                                     to_chunks(vf, HG_DV), to_chunks(log_f, HG_DK)))
    o = o.transpose(1, 0, 3, 2, 4).reshape(B, n_chunks * CHUNK, HG_HEADS, HG_DV)[:, pad:]
    o = o * lax.rsqrt(jnp.mean(jnp.square(o), axis=-1, keepdims=True) + RMS_EPS) * norm_g.astype(f32)
    o = o.reshape(B, L, HG_V_WIDTH) * jax.nn.silu(g_out.astype(f32))
    return o.astype(q.dtype)

def causal_depthwise_conv(x, w, b):
    y = lax.conv_general_dilated(x, w[:, None, :], window_strides=(1,), padding=[(CONV_W - 1, 0)],
                                 dimension_numbers=('NWC', 'WIO', 'NWC'), feature_group_count=x.shape[-1])
    return y + b

def block_diag_linear(x, w, b):
    xb = x.reshape(x.shape[:-1] + (LRU_BLOCKS, LRU_BLOCK))
    return jnp.einsum('blnc,ncd->blnd', xb, w).reshape(x.shape) + b

def rg_lru(x, w_a, b_a, w_x, b_x, lam):
    f32 = jnp.float32
    r = jax.nn.sigmoid(block_diag_linear(x, w_a, b_a).astype(f32))
    i = jax.nn.sigmoid(block_diag_linear(x, w_x, b_x).astype(f32))
    log_a = -LRU_C * r * jax.nn.softplus(-lam.astype(f32))
    a = jnp.exp(log_a)
    u = jnp.sqrt(-jnp.expm1(2.0 * log_a)) * (i * x.astype(f32))

    def combine(c1, c2):
        a1, u1 = c1
        a2, u2 = c2
        return a1 * a2, a2 * u1 + u2

    _, h = lax.associative_scan(combine, (a, u), axis=1)
    return h.astype(x.dtype)

def hybrid_mixer(h, w_in, b_in, lb, hg_norm_g, conv_w, conv_b, lru_wa, lru_ba, lru_wx, lru_bx, lru_lambda, w_out):
    proj = h @ w_in + b_in
    offs = np.cumsum(SPLIT_SIZES)[:-1].tolist()
    q, f_pre, v, g_out, lru_x, lru_g, gate_hg, gate_lru = jnp.split(proj, offs, axis=-1)
    y_hg = hgrn2_mixer(q, f_pre, v, g_out, lb, hg_norm_g)
    y_lru = rg_lru(causal_depthwise_conv(lru_x, conv_w, conv_b), lru_wa, lru_ba, lru_wx, lru_bx,
                   lru_lambda) * jax.nn.gelu(lru_g)
    merged = jax.nn.sigmoid(gate_hg) * y_hg + jax.nn.sigmoid(gate_lru) * y_lru
    return merged @ w_out

def swiglu(x, w_gate, w_up, w_down):
    return (jax.nn.silu(x @ w_gate) * (x @ w_up)) @ w_down

def routed_experts(xt, idx, wts, we_gate, we_up, we_down):
    T, D = xt.shape
    A = T * TOP_K
    n_blocks = -(-A // EXPERT_BLOCK) + N_EXPERTS
    e_flat = idx.reshape(A)
    tok_flat = jnp.arange(A, dtype=jnp.int32) // TOP_K
    order = jnp.argsort(e_flat)
    e_sorted = e_flat[order]
    counts = jnp.bincount(e_flat, length=N_EXPERTS)
    starts = jnp.cumsum(counts) - counts
    padded = (counts + EXPERT_BLOCK - 1) // EXPERT_BLOCK * EXPERT_BLOCK
    pad_ends = jnp.cumsum(padded)
    dest = (pad_ends - padded)[e_sorted] + jnp.arange(A, dtype=counts.dtype) - starts[e_sorted]
    buf_tok = jnp.full((n_blocks * EXPERT_BLOCK,), T, jnp.int32).at[dest].set(tok_flat[order])
    buf_w = jnp.zeros((n_blocks * EXPERT_BLOCK,), wts.dtype).at[dest].set(wts.reshape(A)[order])
    block_start = jnp.arange(n_blocks, dtype=pad_ends.dtype) * EXPERT_BLOCK
    block_expert = jnp.minimum(jnp.searchsorted(pad_ends, block_start, side='right'), N_EXPERTS - 1)
    x_pad = jnp.concatenate([xt, jnp.zeros((1, D), xt.dtype)], axis=0)

    def block_step(acc, inp):
        e, tok_b, w_b = inp
        y_b = swiglu(x_pad[tok_b], we_gate[e], we_up[e], we_down[e])
        return acc.at[tok_b].add(y_b * w_b[:, None]), None

    acc, _ = lax.scan(block_step, jnp.zeros((T + 1, D), xt.dtype),
                      (block_expert, buf_tok.reshape(n_blocks, EXPERT_BLOCK),
                       buf_w.reshape(n_blocks, EXPERT_BLOCK)))
    return acc[:T]

def moe_ffn(h, router_w, router_bias, we_gate, we_up, we_down, ws_gate, ws_up, ws_down):
    B, L, D = h.shape
    xt = h.reshape(B * L, D)
    scores = jax.nn.sigmoid((xt @ router_w).astype(jnp.float32))
    _, idx = lax.top_k(scores + router_bias.astype(jnp.float32), TOP_K)
    s_sel = jnp.take_along_axis(scores, idx, axis=-1)
    wts = s_sel / jnp.sum(s_sel, axis=-1, keepdims=True) * ROUTED_SCALE
    y = routed_experts(xt, idx, wts.astype(xt.dtype), we_gate, we_up, we_down) + swiglu(xt, ws_gate, ws_up, ws_down)
    return y.reshape(B, L, D)

def setup_inputs(seed: int = 0) -> dict:
    key = jax.random.key(seed)
    ks = jax.random.split(key, 28)
    f32 = jnp.float32

    def nrm(k, shape, scale):
        return jax.random.normal(k, shape, f32) * scale

    d_inv = D_MODEL ** -0.5
    u2 = jax.random.uniform(ks[14], (DEPTH, LRU_WIDTH), f32, 0.81, 0.998)
    log_sig = 0.5 * jnp.log(u2) / LRU_C
    lru_lambda = log_sig - jnp.log(-jnp.expm1(log_sig))
    return {
        'x': nrm(ks[0], (BATCH, SEQ, D_MODEL), 1.0),
        'meta_tokens': nrm(ks[1], (N_META, D_MODEL), 1.0),
        'ln_in_g': 1.0 + nrm(ks[2], (D_MODEL,), 0.02),
        'ln_in_b': nrm(ks[3], (D_MODEL,), 0.02),
        'w_in': nrm(ks[4], (DEPTH, D_MODEL, IN_COLS), d_inv),
        'b_in': nrm(ks[5], (DEPTH, IN_COLS), 0.02),
        'hg_lb_logits': nrm(ks[6], (DEPTH + 1, HG_K_WIDTH), 0.5),
        'hg_norm_g': 1.0 + nrm(ks[7], (DEPTH, HG_DV), 0.02),
        'conv_w': nrm(ks[8], (DEPTH, CONV_W, LRU_WIDTH), CONV_W ** -0.5),
        'conv_b': nrm(ks[9], (DEPTH, LRU_WIDTH), 0.02),
        'lru_wa': nrm(ks[10], (DEPTH, LRU_BLOCKS, LRU_BLOCK, LRU_BLOCK), LRU_BLOCK ** -0.5),
        'lru_ba': nrm(ks[11], (DEPTH, LRU_WIDTH), 0.02),
        'lru_wx': nrm(ks[12], (DEPTH, LRU_BLOCKS, LRU_BLOCK, LRU_BLOCK), LRU_BLOCK ** -0.5),
        'lru_bx': nrm(ks[13], (DEPTH, LRU_WIDTH), 0.02),
        'lru_lambda': lru_lambda,
        'w_out': nrm(ks[15], (DEPTH, D_MODEL, D_MODEL), DEEPNORM_BETA * d_inv),
        'ln1_g': 1.0 + nrm(ks[16], (DEPTH, D_MODEL), 0.02),
        'ln1_b': nrm(ks[17], (DEPTH, D_MODEL), 0.02),
        'router_w': nrm(ks[18], (DEPTH, D_MODEL, N_EXPERTS), d_inv),
        'router_bias': nrm(ks[19], (DEPTH, N_EXPERTS), 0.01),
        'we_gate': nrm(ks[20], (DEPTH, N_EXPERTS, D_MODEL, D_EXPERT), d_inv),
        'we_up': nrm(ks[21], (DEPTH, N_EXPERTS, D_MODEL, D_EXPERT), d_inv),
        'we_down': nrm(ks[22], (DEPTH, N_EXPERTS, D_EXPERT, D_MODEL), DEEPNORM_BETA * D_EXPERT ** -0.5),
        'ws_gate': nrm(ks[23], (DEPTH, D_MODEL, D_SHARED), d_inv),
        'ws_up': nrm(ks[24], (DEPTH, D_MODEL, D_SHARED), d_inv),
        'ws_down': nrm(ks[25], (DEPTH, D_SHARED, D_MODEL), DEEPNORM_BETA * D_SHARED ** -0.5),
        'ln2_g': 1.0 + nrm(ks[26], (DEPTH, D_MODEL), 0.02),
        'ln2_b': nrm(ks[27], (DEPTH, D_MODEL), 0.02),
    }

def reference(x, meta_tokens, ln_in_g, ln_in_b, w_in, b_in, hg_lb_logits, hg_norm_g, conv_w, conv_b,
              lru_wa, lru_ba, lru_wx, lru_bx, lru_lambda, w_out, ln1_g, ln1_b, router_w, router_bias,
              we_gate, we_up, we_down, ws_gate, ws_up, ws_down, ln2_g, ln2_b):
    B = x.shape[0]
    meta = jnp.broadcast_to(meta_tokens[None].astype(x.dtype), (B, N_META, D_MODEL))
    h = layer_norm(jnp.concatenate([meta, x], axis=1), ln_in_g, ln_in_b)
    lower_bounds = jnp.cumsum(jax.nn.softmax(hg_lb_logits.astype(jnp.float32), axis=0), axis=0)
    for l in range(DEPTH):
        mix = hybrid_mixer(h, w_in[l], b_in[l], lower_bounds[l], hg_norm_g[l], conv_w[l], conv_b[l],
                           lru_wa[l], lru_ba[l], lru_wx[l], lru_bx[l], lru_lambda[l], w_out[l])
        h = layer_norm(DEEPNORM_ALPHA * h + mix, ln1_g[l], ln1_b[l])
        ffn = moe_ffn(h, router_w[l], router_bias[l], we_gate[l], we_up[l], we_down[l],
                      ws_gate[l], ws_up[l], ws_down[l])
        h = layer_norm(DEEPNORM_ALPHA * h + ffn, ln2_g[l], ln2_b[l])
    return h[:, N_META:]


_drawn_inputs = setup_inputs


def setup_inputs(seed=0):
    import zlib

    import numpy as np

    out = dict(_drawn_inputs(seed))
    spreads = {}
    factors = {'hg_norm_g': 2.883, 'lru_ba': 22.465, 'lru_bx': 16.439, 'ln2_g': 7.858, 'ln2_b': 8.743}
    for name, (base, spread) in spreads.items():
        noise = np.random.default_rng([zlib.crc32(name.encode()), seed]).standard_normal(out[name].shape)
        drawn = base * np.exp(spread * noise) if base else spread * noise
        out[name] = jnp.asarray(drawn.astype(out[name].dtype))
    for name, factor in factors.items():
        out[name] = (out[name] * factor).astype(out[name].dtype)
    return out
```

```python
from contextlib import ExitStack

import numpy as np
import concourse.bass as bass
from concourse import mybir

P = 128
D = 1024
KB = D // P
META = 16
T = 512
TA = META + T
TT = T // P
HEADS = 8
GROUPS = 8
GQ, GF, GV, GO, GX, GL, GHG, GLRU = range(8)
W_ORDER = (GF, GQ, GV, GX, GO, GL, GHG, GLRU)
CHUNK = 64
SUB = 16
NSUB = CHUNK // SUB
NCH = T // CHUNK
CONV_W = 4
E = 64
TOP_K = 6
F = 256
SLOTS = 64
EXTRA = T * TOP_K // SLOTS
ITEMS = E + EXTRA
QUAD = 4
QUADS_MAX = ITEMS // QUAD
CHUNK_W = 2048
CHUNKS = 3
RAW = 6
FAR = 4096.0
ALPHA = 2.0 ** 0.25
LN_EPS, RMS_EPS = 1e-5, 1e-6
ROUTED_SCALE = 2.5
GELU_A, GELU_B = 0.044715, 2.0 * 0.7978845608028654
(C_BQ, C_BF, C_BG, C_BX, C_BL, C_BHG, C_BLRU, C_NG, C_W0, C_W1, C_W2, C_W3, C_CB, C_BA,
 C_BI) = range(15)
NCOL = 15

ALU = mybir.AluOpType
ACT = mybir.ActivationFunctionType
F32 = mybir.dt.float32
F32R = mybir.dt.float32r
BF16 = mybir.dt.bfloat16
I32 = mybir.dt.int32
AX = mybir.AxisListType.X


class Steps:

    def __init__(self, eng, sem, base=0):
        self.eng, self.sem, self.base, self.n = eng, sem, base, 0

    def __call__(self, ins):
        self.n += 1
        ins.then_inc(self.sem, 1)
        self.eng.wait_ge(self.sem, self.base + self.n)

    def add(self, ins):
        self.n += 1
        ins.then_inc(self.sem, 1)

    def sync(self):
        self.eng.wait_ge(self.sem, self.base + self.n)


def program(nc, a, out, stop=9, dbg=None):
    with ExitStack() as whole:
        sems = {}

        def sem(name):
            if name not in sems:
                sems[name] = whole.enter_context(nc.semaphore(name))
            return sems[name]

        top = [(nc.sbuf_base + 63) // 64 * 64]

        def sb(name, shape, dt=F32, at=None):
            size = int(np.prod(shape[1:])) * (2 if dt == BF16 else 4)
            if at is None:
                at = top[0]
                top[0] += (size + 63) // 64 * 64
                assert top[0] <= nc.sbuf_usable_end, (name, top[0])
            return nc.alloc_sbuf_tensor_at(name, shape, dt, offset=at)

        pair = [whole.enter_context(nc.psum_tensor(f"pair{i}", [P, 1024], F32)) for i in range(4)]
        banks = [pair[i // 2][:, (i % 2) * 512:(i % 2) * 512 + 512] for i in range(8)]

        mem = {}
        mem["ident"] = sb("ident", [P, P])
        mem["ones"] = sb("ones", [P, P])
        mem["acc"] = sb("acc", [P, TT, D])
        raw_at = top[0]
        mem["raw"] = sb("raw", [P, RAW, CHUNK_W])
        mem["merged"] = sb("merged", [P, HEADS, T], at=raw_at + (RAW - 2) * CHUNK_W * 4)
        persist = top[0]
        top[0] = raw_at
        front(nc, a, sem, sb, banks, mem, stop, dbg, top)
        if stop <= 2:
            return
        top[0] = persist
        mem["x_hi"] = sb("x_hi", [P, TT, KB, P], F32R)
        mem["x_lo"] = sb("x_lo", [P, TT, KB, P], F32R)
        mem["slot_of"] = sb("slot_of", [P, ITEMS + QUAD, TT])
        mem["weight_of"] = sb("weight_of", [P, ITEMS, TT, 3], BF16)
        mem["expert_of"] = sb("expert_of", [1, ITEMS], I32)
        mem["quads"] = sb("quads", [1, 1], I32)
        mem["iota"] = sb("iota", [P, SLOTS])
        phase = top[0]
        out_and_route(nc, a, sem, sb, banks, pair, mem, stop, dbg)
        if stop <= 3:
            return
        top[0] = phase
        experts(nc, a, sem, sb, banks, pair, mem, stop, dbg)
        if stop <= 4:
            dump(nc, sem, dbg, mem["acc"][:, :, :])
            return
        top[0] = phase
        output_norm(nc, a, sem, sb, mem, out)


def front(nc, a, sem, sb, banks, mem, stop, dbg, top):
    ident, ones, h_res, merged = mem["ident"], mem["ones"], mem["acc"], mem["merged"]
    low = [top[0]]
    top[0] += RAW * CHUNK_W * 4

    def sb_low(name, shape):
        at = low[0]
        low[0] += int(np.prod(shape[1:])) * 4
        assert low[0] <= top_low
        return sb(name, shape, at=at)

    top_low = low[0] + (RAW - 2) * CHUNK_W * 4
    hT = sb("hT", [P, KB, TA])
    w = [sb(f"w{s}", [P, GROUPS, KB, P]) for s in range(2)]
    par = [sb(f"par{s}", [P, NCOL]) for s in range(2)]
    lw = [sb(f"lw{s}", [P, 2, P]) for s in range(2)]
    vb = [sb(f"vb{s}", [1, P]) for s in range(2)]
    cols = sb("cols", [P, 2, KB])
    cmask = sb("cmask", [P, CHUNK])
    reset = sb("reset", [P, TA])

    def load_head(sp, j, s):
        for n in range(0, GROUPS, 2):
            sp.dma_start(w[s][:, n:n + 2], a["w_in"][j, :, n:n + 2]).then_inc(sem(f"w_here_{n // 2}_{s}"), 16)
            if n == 0:
                sp.dma_start(par[s][:], a["head_cols"][j]).then_inc(sem(f"par_here_{s}"), 16)
                sp.dma_start(vb[s][:], a["v_bias"][j]).then_inc(sem(f"par_here_{s}"), 16)
                sp.dma_start(lw[s][:], a["lru_w"][j]).then_inc(sem(f"lw_here_{s}"), 16)

    both = top[0]
    with nc.Block() as block:
        xin = sb("xin", [P, TT + 1, D])
        stats = sb("stats", [P, TT + 1, 2, 6])
        mv = sb("mv", [P, TT + 1, 2])
        rs = sb("rs", [P, TT + 1, 2])
        g_row = sb("g_row", [P, D])
        b_row = sb("b_row", [P, D])
        x_here = [sem(f"x_here{t}") for t in range(TT + 1)]
        consts, rows_here = sem("consts_here"), sem("rows_here")
        var_ready, std_ready, xn_ready = sem("var_ready"), sem("std_ready"), sem("xn_ready")
        tr_ready, tr_taken = sem("tr_ready"), sem("tr_taken")

        @block.sync
        def _(sp):
            for t in range(TT):
                sp.dma_start(xin[:, t], a["x"][t * P:(t + 1) * P]).then_inc(x_here[t], 16)
            sp.dma_start(xin[0:META, TT], a["meta"]).then_inc(x_here[TT], 16)
            sp.dma_start(ident[:], a["ident"]).then_inc(consts, 16)
            sp.dma_start(cols[:, 0:2], a["norm_cols"]).then_inc(consts, 16)
            sp.dma_start(cmask[:], a["cmask"]).then_inc(consts, 16)
            sp.dma_start(reset[:], a["reset"]).then_inc(consts, 16)
            load_head(sp, 0, 0)
            sp.dma_start(g_row[:], a["norm_rows"][0:1].broadcast_to([P, D])).then_inc(rows_here, 16)
            sp.dma_start(b_row[:], a["norm_rows"][1:2].broadcast_to([P, D])).then_inc(rows_here, 16)

        @block.vector
        def _(v):
            st = Steps(v, sem("dve_step"))
            st.add(v.memset(ones[:], 1.0))
            for t in range(TT + 1):
                n = P if t < TT else META
                v.wait_ge(x_here[t], 16)
                st.add(v.bn_stats(stats[0:n, t, 0], xin[0:n, t, 0:512]))
                st(v.bn_stats(stats[0:n, t, 1], xin[0:n, t, 512:1024]))
                st(v.bn_aggr(mv[0:n, t], stats[0:n, t]))
                v.tensor_scalar(rs[0:n, t, 0:1], mv[0:n, t, 1:2], LN_EPS, None, ALU.add).then_inc(var_ready, 1)
            for t in range(TT + 1):
                n = P if t < TT else META
                v.wait_ge(std_ready, t + 1)
                st(v.reciprocal(rs[0:n, t, 0:1], rs[0:n, t, 1:2]))
                v.tensor_scalar(xin[0:n, t], xin[0:n, t], mv[0:n, t, 0:1], rs[0:n, t, 0:1],
                                ALU.subtract, ALU.mult).then_inc(xn_ready, 1)
            v.wait_ge(consts, 64)
            for k in range(KB):
                v.wait_ge(tr_ready, k + 1)
                v.tensor_scalar(hT[:, k, META:TA], banks[k % 4][:, 0:T], cols[:, 0, k:k + 1],
                                cols[:, 1, k:k + 1], ALU.mult, ALU.add).then_inc(tr_taken, 1)
            v.wait_ge(tr_ready, KB + 1)
            for k in range(KB):
                v.tensor_scalar(hT[:, k, 0:META], banks[4][:, k * META:(k + 1) * META], cols[:, 0, k:k + 1],
                                cols[:, 1, k:k + 1], ALU.mult, ALU.add)

        @block.scalar
        def _(act):
            for t in range(TT + 1):
                n = P if t < TT else META
                act.wait_ge(var_ready, t + 1)
                act.activation(rs[0:n, t, 1:2], rs[0:n, t, 0:1], ACT.Sqrt).then_inc(std_ready, 1)

        @block.tensor
        def _(pe):
            pe.wait_ge(consts, 64)
            pe.wait_ge(xn_ready, TT + 1)
            for k in range(KB):
                if k >= 4:
                    pe.wait_ge(tr_taken, k - 3)
                for t in range(TT):
                    last = pe.transpose(banks[k % 4][:, t * P:(t + 1) * P], xin[:, t, k::KB], ident[:])
                last.then_inc(tr_ready, 1)
            for k in range(KB):
                last = pe.transpose(banks[4][:, k * META:(k + 1) * META], xin[0:META, TT, k::KB],
                                    ident[0:META, 0:META])
            last.then_inc(tr_ready, 1)

        @block.gpsimd
        def _(pool):
            gst = Steps(pool, sem("pool_step"))
            pool.wait_ge(rows_here, 32)
            for t in range(TT):
                pool.wait_ge(xn_ready, t + 1)
                gst(pool.tensor_tensor(h_res[:, t], xin[:, t], g_row[:], ALU.mult))
                gst(pool.tensor_tensor(h_res[:, t], h_res[:, t], b_row[:], ALU.add))

    if stop <= 1:
        dump(nc, sem, dbg, hT[:, :, :])
        return

    top[0] = both
    with nc.Block() as block:
        all_cols = sb("all_cols", [P, 3, HEADS])
        lam = sb("lam", [P, 6, HEADS])
        derived = sb("derived", [P, HEADS, 4])
        own = [sb(f"own{s}", [P, 4]) for s in range(2)]
        sig_f = sb_low("sig_f", [P, TA])
        f = sb_low("f", [P, TA])
        kk = sb_low("kk", [P, TA])
        b = sb_low("b", [P, TA])
        q = sb_low("q", [P, T])
        eq = sb_low("eq", [P, T])
        eb = sb_low("eb", [P, T])
        q_in = sb("q_in", [P, T])
        q_st = sb("q_st", [P, T])
        k_in = sb_low("k_in", [P, NSUB, NCH, CHUNK])
        k_st = sb("k_st", [P, TA])
        kT = sb("kT", [P, TT, P])
        kTm = sb("kTm", [META, P])
        vt = sb("vt", [P, TT, P])
        vm = sb("vm", [META, P])
        sc = sb("sc", [P, TT, CHUNK])
        S = sb_low("S", [P, NCH, P])
        o2 = sb("o2", [P, T])
        rms = sb("rms", [P, T])
        y = sb("y", [P, T])
        xr = sb("xr", [P, CONV_W - 1 + TA])
        xc = sb("xc", [P, TA])
        rr = sb("rr", [P, TA])
        ii = sb("ii", [P, TA])
        la = sb("la", [P, TA])
        pp = sb("pp", [P, TA])
        u = sb("u", [P, TA])
        gx = sb("gx", [P, T])
        gt = sb("gt", [P, T])
        sg = [sb(f"sg{i}", [P, T]) for i in range(3)]
        eps = sb("eps", [P, 1])

        BF_, BQ_, BV_, BX_ = banks[0], banks[1], banks[2], banks[3]
        B4, B7 = banks[6], banks[7]
        B5, B6 = banks[4], banks[5]
        halves = lambda t: t[:, :].rearrange("p (t h s) -> p t h s", t=TT, h=2)
        of_half = lambda bank: bank[:, 0:TT * CHUNK].rearrange("p (t s) -> p t s", t=TT)
        chunked = lambda t: t.rearrange("p (c s) -> p c s", c=NCH)

        per_head = ("f_done q_done v_done x_done o_done l_done hg_done lru_done kt_done ri_done sc_done "
                    "kv_done out_done rms_done").split()
        pe_sem = {n: sem("pe_" + n) for n in per_head}

        @block.sync
        def _(sp):
            sp.dma_start(all_cols[:], a["all_cols"]).then_inc(sem("all_cols_here"), 16)
            load_head(sp, 1, 1)
            with sp.Fori(1, HEADS // 2) as r:
                for s in range(2):
                    sp.wait_ge(sem("merged_done"), 2 * r + s - 1)
                    load_head(sp, 2 * r + s, s)

        @block.tensor
        def _(pe):
            for name in ("o_taken", "ri_taken", "l_taken", "hg_taken", "lru_taken"):
                pe.sem_inc(sem(name), 1)
            with pe.Fori(0, HEADS // 2) as r:
                for s in range(2):
                    j = 2 * r + s

                    def project(bank, g, meta_at=None, after=None):
                        n = W_ORDER.index(g)
                        pe.wait_ge(sem(f"w_here_{n // 2}_{s}"), 16 * r + 16)
                        for k in range(KB):
                            last = pe.matmul(bank[:, 0:T], w[s][:, n, k], hT[:, k, META:TA],
                                             start=(k == 0), stop=(k == KB - 1))
                        if meta_at is not None:
                            if after:
                                pe.wait_ge(sem(after), j + 1)
                            for k in range(KB):
                                last = pe.matmul(B7[:, meta_at:meta_at + META], w[s][:, n, k],
                                                 hT[:, k, 0:META], start=(k == 0), stop=(k == KB - 1))
                        return last

                    pe.wait_ge(sem("o_taken"), j + 1)
                    pe.wait_ge(sem("ri_taken"), j + 1)
                    project(BF_, GF, 0).then_inc(pe_sem["f_done"], 1)
                    pe.wait_ge(sem("l_taken"), j + 1)
                    project(BQ_, GQ).then_inc(pe_sem["q_done"], 1)

                    pe.wait_ge(sem("hg_taken"), j + 1)
                    pe.wait_ge(sem(f"w_here_{W_ORDER.index(GV) // 2}_{s}"), 16 * r + 16)
                    pe.wait_ge(sem(f"par_here_{s}"), 32 * r + 32)
                    for t in range(TT + 1):
                        n = P if t < TT else META
                        if t == TT:
                            pe.wait_ge(sem("f_taken"), j + 1)
                        o = BV_[:, t * P:(t + 1) * P] if t < TT else B7[0:META, 128:256]
                        c0 = META + t * P if t < TT else 0
                        for k in range(KB):
                            pe.matmul(o, hT[:, k, c0:c0 + n], w[s][:, W_ORDER.index(GV), k], start=(k == 0), stop=False)
                        last = pe.matmul(o, ones[0:1, 0:n], vb[s][:], start=False, stop=True)
                    last.then_inc(pe_sem["v_done"], 1)
                    pe.wait_ge(sem("lru_taken"), j + 1)
                    project(BX_, GX, 16, "v_taken").then_inc(pe_sem["x_done"], 1)
                    pe.wait_ge(sem("f_taken"), j + 1)
                    project(BF_, GO).then_inc(pe_sem["o_done"], 1)

                    pe.wait_ge(sem("qk_ready"), j + 1)
                    for t in range(TT):
                        pe.transpose(B4[:, t * P:(t + 1) * P], k_st[:, META + t * P:META + (t + 1) * P], ident[:])
                    pe.wait_ge(sem("x_taken"), j + 1)
                    pe.transpose(B7[0:META, 256:384], k_st[:, 0:META], ident[:]).then_inc(pe_sem["kt_done"], 1)
                    pe.wait_ge(sem("q_taken"), j + 1)
                    project(BQ_, GL).then_inc(pe_sem["l_done"], 1)

                    pe.wait_ge(sem("xc_ready"), j + 1)
                    pe.wait_ge(sem(f"lw_here_{s}"), 16 * r + 16)
                    pe.wait_ge(sem("kt_taken"), j + 1)
                    for i, bank in enumerate((B5, B6)):
                        pe.matmul(bank[:, 0:T], lw[s][:, i], xc[:, META:TA], start=True, stop=True)
                        last = pe.matmul(B7[:, 32 + 16 * i:48 + 16 * i], lw[s][:, i], xc[:, 0:META],
                                         start=True, stop=True)
                    last.then_inc(pe_sem["ri_done"], 1)

                    pe.wait_ge(sem("kt_taken"), j + 1)
                    for c in range(NCH):
                        t, h0 = c // 2, CHUNK * (c % 2)
                        for i in range(NSUB):
                            last = pe.matmul(B4[h0:h0 + CHUNK, t * CHUNK + i * SUB:t * CHUNK + (i + 1) * SUB],
                                             k_in[:, i, c], q_in[:, c * CHUNK + i * SUB:c * CHUNK + (i + 1) * SUB],
                                             start=True, stop=True)
                    last.then_inc(pe_sem["sc_done"], 1)
                    pe.wait_ge(sem("ri_taken"), j + 2)
                    pe.matmul(B7[:, 384:512], kTm[:], vm[:], start=True, stop=True)
                    for c in range(NCH - 1):
                        t, h0 = c // 2, CHUNK * (c % 2)
                        last = pe.matmul((B5, B6)[c % 2][:, t * P:(t + 1) * P], kT[h0:h0 + CHUNK, t],
                                         vt[h0:h0 + CHUNK, t], start=True, stop=True)
                    last.then_inc(pe_sem["kv_done"], 1)
                    pe.wait_ge(sem("v_taken"), j + 1)
                    project(BV_, GHG).then_inc(pe_sem["hg_done"], 1)

                    pe.wait_ge(sem("sc_ready"), j + 1)
                    pe.wait_ge(sem("S_ready"), j + 1)
                    for c in range(NCH):
                        t, h0 = c // 2, CHUNK * (c % 2)
                        o = (B4, B6)[c % 2][:, t * CHUNK:(t + 1) * CHUNK]
                        pe.matmul(o, vt[h0:h0 + CHUNK, t], sc[h0:h0 + CHUNK, t], start=True, stop=False)
                        last = pe.matmul(o, S[:, c], q_st[:, c * CHUNK:(c + 1) * CHUNK], start=False, stop=True)
                    last.then_inc(pe_sem["out_done"], 1)
                    pe.wait_ge(sem("x_taken"), j + 1)
                    project(BX_, GLRU).then_inc(pe_sem["lru_done"], 1)
                    pe.wait_ge(sem("o2_ready"), j + 1)
                    pe.matmul(B5[:, 0:T], ones[:], o2[:], start=True, stop=True).then_inc(pe_sem["rms_done"], 1)

        @block.scalar
        def _(act):
            act.wait_ge(sem("eps_ready"), 1)
            act.wait_ge(sem("lam_ready"), 1)
            act.activation(lam[:, 1], lam[:, 0], ACT.Exp)
            act.activation(derived[:, :, 0], derived[:, :, 1], ACT.Sigmoid).then_inc(sem("elam_ready"), 1)
            with act.Fori(0, HEADS // 2) as r:
                for s in range(2):
                    j = 2 * r + s
                    c = lambda n: par[s][:, n:n + 1]
                    act.wait_ge(sem(f"par_here_{s}"), 32 * r + 32)
                    act.wait_ge(pe_sem["f_done"], j + 1)
                    act.activation(sig_f[:, 0:META], B7[:, 0:META], ACT.Sigmoid, bias=c(C_BF))
                    act.activation(sig_f[:, META:TA], BF_[:, 0:T], ACT.Sigmoid, bias=c(C_BF)).then_inc(sem("f_taken"), 1)
                    act.wait_ge(pe_sem["q_done"], j + 1)
                    act.activation(eq[:], BQ_[:, 0:T], ACT.Sigmoid, bias=c(C_BQ)).then_inc(sem("sigq_ready"), 1)
                    act.wait_ge(sem("f_ready"), j + 1)
                    act.activation(u[:], f[:], ACT.Ln).then_inc(sem("lf_ready"), 1)
                    act.wait_ge(pe_sem["v_done"], j + 1)
                    act.activation(vm[:], B7[0:META, 128:256], ACT.Copy)
                    act.activation(vt[:].rearrange("p t c -> p (t c)"), BV_[:, 0:T], ACT.Copy).then_inc(sem("v_taken"), 1)
                    act.wait_ge(pe_sem["x_done"], j + 1)
                    act.activation(xr[:, 3:3 + META], B7[:, 16:16 + META], ACT.Identity, bias=c(C_BX))
                    act.activation(xr[:, 3 + META:3 + TA], BX_[:, 0:T], ACT.Identity, bias=c(C_BX)).then_inc(sem("x_taken"), 1)
                    act.wait_ge(sem("args_ready"), j + 1)
                    act.activation(eq[:], eq[:], ACT.Exp)
                    act.activation(eb[:], b[:, META:TA], ACT.Exp)
                    for i in range(NSUB):
                        n = SUB * (i + 1)
                        act.activation(k_in[:, i, :, 0:n], k_in[:, i, :, 0:n], ACT.Exp)
                    act.activation(k_st[:], k_st[:], ACT.Exp).then_inc(sem("exps_ready"), 1)
                    act.wait_ge(pe_sem["o_done"], j + 1)
                    act.activation(sg[0][:], BF_[:, 0:T], ACT.Sigmoid, bias=c(C_BG)).then_inc(sem("sigo_ready"), 1)
                    act.wait_ge(pe_sem["kt_done"], j + 1)
                    act.activation(kTm[:], B7[0:META, 256:384], ACT.Copy)
                    act.activation(kT[:].rearrange("p t c -> p (t c)"), B4[:, 0:T], ACT.Copy).then_inc(sem("kt_taken"), 1)
                    act.wait_ge(pe_sem["l_done"], j + 1)
                    act.activation(gx[:], BQ_[:, 0:T], ACT.Identity, bias=c(C_BL)).then_inc(sem("l_taken"), 1)
                    act.wait_ge(pe_sem["ri_done"], j + 1)
                    act.activation(rr[:, 0:META], B7[:, 32:48], ACT.Sigmoid, bias=c(C_BA))
                    act.activation(rr[:, META:TA], B5[:, 0:T], ACT.Sigmoid, bias=c(C_BA))
                    act.activation(ii[:, 0:META], B7[:, 48:64], ACT.Sigmoid, bias=c(C_BI))
                    act.activation(ii[:, META:TA], B6[:, 0:T], ACT.Sigmoid, bias=c(C_BI)).then_inc(sem("ri_taken"), 1)
                    act.wait_ge(sem("ri_taken"), j + 2)
                    act.wait_ge(sem("gelu_arg"), j + 1)
                    act.activation(gt[:], gt[:], ACT.Sigmoid, scale=GELU_B).then_inc(sem("gelu_sig"), 1)
                    act.activation(la[:], rr[:], ACT.Exp, scale=own[s][:, 2:3])
                    act.activation(pp[:], rr[:], ACT.Tanh, scale=own[s][:, 3:4]).then_inc(sem("a_ready"), 1)
                    act.wait_ge(pe_sem["hg_done"], j + 1)
                    act.activation(sg[1][:], BV_[:, 0:T], ACT.Sigmoid, bias=c(C_BHG)).then_inc(sem("hg_taken"), 1)
                    act.wait_ge(pe_sem["out_done"], j + 1)
                    act.activation(halves(o2)[:, :, 0], of_half(B4), ACT.Square)
                    act.activation(halves(o2)[:, :, 1], of_half(B6), ACT.Square).then_inc(sem("o2_ready"), 1)
                    act.wait_ge(pe_sem["lru_done"], j + 1)
                    act.activation(sg[2][:], BX_[:, 0:T], ACT.Sigmoid, bias=c(C_BLRU)).then_inc(sem("lru_taken"), 1)
                    act.wait_ge(sem("u2_ready"), j + 1)
                    act.activation(pp[:], pp[:], ACT.Sqrt, scale=2.0).then_inc(sem("u_root"), 1)
                    act.wait_ge(pe_sem["rms_done"], j + 1)
                    act.activation(rms[:], B5[:, 0:T], ACT.Sqrt, bias=eps[:], scale=1.0 / P).then_inc(sem("rms_ready"), 1)

        @block.vector
        def _(v):
            N = 42
            st0 = Steps(v, sem("dve2_step"))
            st0.add(v.memset(k_in[:], 0.0))
            st0.add(v.memset(xr[:, 0:3], 0.0))
            v.memset(eps[:], RMS_EPS).then_inc(sem("eps_ready"), 1)
            v.wait_ge(sem("all_cols_here"), 16)
            st0(v.tensor_scalar(lam[:, 5], all_cols[:, 0], -1.0, None, ALU.mult))
            st0.add(v.tensor_scalar(lam[:, 2], lam[:, 5], 0.0, None, ALU.max))
            st0.add(v.tensor_tensor(derived[:, :, 1], all_cols[:, 1], all_cols[:, 2], ALU.subtract))
            st0(v.tensor_tensor(lam[:, 0], lam[:, 5], all_cols[:, 0], ALU.min))
            v.sem_inc(sem("lam_ready"), 1)
            v.wait_ge(sem("elam_ready"), 1)
            e_, t_, s2, ac = lam[:, 1], lam[:, 3], lam[:, 4], lam[:, 5]
            st0.add(v.tensor_scalar(derived[:, :, 1], derived[:, :, 0], -1.0, 1.0, ALU.mult, ALU.add))
            st0(v.tensor_scalar(t_, e_, 2.0, None, ALU.add))
            st0(v.reciprocal(t_, t_))
            st0(v.tensor_tensor(t_, t_, e_, ALU.mult))
            st0(v.tensor_tensor(s2, t_, t_, ALU.mult))
            st0(v.tensor_scalar(ac, s2, 2.0 / 15, 2.0 / 13, ALU.mult, ALU.add))
            for n in (11, 9, 7, 5, 3, 1):
                st0(v.tensor_tensor(ac, ac, s2, ALU.mult))
                st0(v.tensor_scalar(ac, ac, 2.0 / n, None, ALU.add))
            st0(v.tensor_tensor(ac, ac, t_, ALU.mult))
            st0(v.tensor_tensor(ac, ac, lam[:, 2], ALU.add))
            st0.add(v.tensor_scalar(derived[:, :, 2], ac, -8.0, None, ALU.mult))
            st0(v.tensor_scalar(derived[:, :, 3], ac, 8.0, None, ALU.mult))
            with v.Fori(0, HEADS // 2) as r:
                for s in range(2):
                    j = 2 * r + s
                    st = Steps(v, sem("dve2_step"), N * j + st0.n)
                    c = lambda n: par[s][:, n:n + 1]
                    v.wait_ge(sem(f"par_here_{s}"), 32 * r + 32)
                    st(v.tensor_copy(own[s][:], derived[:, bass.ds(j, 1)].rearrange("p a n -> p (a n)")))
                    v.wait_ge(sem("f_taken"), j + 1)
                    st(v.tensor_scalar(f[:], sig_f[:], own[s][:, 1:2], own[s][:, 0:1], ALU.mult, ALU.add))
                    v.tensor_scalar(kk[:], f[:], -1.0, 1.0, ALU.mult, ALU.add).then_inc(sem("f_ready"), 1)
                    v.wait_ge(sem("sigq_ready"), j + 1)
                    v.scalar_tensor_tensor(q[:], BQ_[:, 0:T], c(C_BQ), eq[:], ALU.add, ALU.mult).then_inc(sem("q_taken"), 1)
                    v.wait_ge(sem("lf_ready"), j + 1)
                    st(v.tensor_tensor_scan(b[:], reset[:], u[:], 0.0, ALU.mult, ALU.add))
                    b4 = b[:, META:TA].rearrange("p (c i s) -> p c i s", c=NCH, i=NSUB)
                    mid = b4[:, :, :, SUB // 2 - 1:SUB // 2]
                    v.wait_ge(sem("q_taken"), j + 1)
                    st.add(v.tensor_tensor(eq[:].rearrange("p (c i s) -> p (c i) s", c=NCH, i=NSUB),
                                           b4.rearrange("p c i s -> p (c i) s"),
                                           mid.rearrange("p c i s -> p (c i) s").broadcast_to([P, NCH * NSUB, SUB]),
                                           ALU.subtract))
                    bc = chunked(b[:, META:TA])
                    for i in range(NSUB):
                        n = SUB * (i + 1)
                        st.add(v.tensor_tensor(k_in[:, i, :, 0:n], mid[:, :, i].broadcast_to([P, NCH, n]),
                                               bc[:, :, 0:n], ALU.subtract))
                    st.add(v.tensor_tensor(chunked(k_st[:, META:TA]), bc[:, :, CHUNK - 1:CHUNK].broadcast_to([P, NCH, CHUNK]),
                                           bc, ALU.subtract))
                    st(v.tensor_tensor(k_st[:, 0:META], b[:, META - 1:META].broadcast_to([P, META]), b[:, 0:META],
                                       ALU.subtract))
                    v.sem_inc(sem("args_ready"), 1)
                    v.wait_ge(sem("x_taken"), j + 1)
                    st(v.tensor_scalar(xc[:], xr[:, 3:3 + TA], c(C_W3), c(C_CB), ALU.mult, ALU.add))
                    for i in range(3):
                        ins = v.scalar_tensor_tensor(xc[:], xr[:, i:i + TA], c(C_W0 + i), xc[:], ALU.mult, ALU.add)
                        if i < 2:
                            st(ins)
                        else:
                            ins.then_inc(sem("xc_ready"), 1)
                    v.wait_ge(sem("exps_ready"), j + 1)
                    st.add(v.tensor_tensor(q_in[:], q[:], eq[:], ALU.mult))
                    st.add(v.tensor_tensor(q_st[:], q[:], eb[:], ALU.mult))
                    kc = chunked(kk[:, META:TA])
                    for i in range(NSUB):
                        n = SUB * (i + 1)
                        st.add(v.tensor_tensor(k_in[:, i, :, 0:n], k_in[:, i, :, 0:n], kc[:, :, 0:n], ALU.mult))
                    st(v.tensor_tensor(k_st[:], k_st[:], kk[:], ALU.mult))
                    v.sem_inc(sem("qk_ready"), 1)
                    v.wait_ge(sem("sigo_ready"), j + 1)
                    v.scalar_tensor_tensor(sg[0][:], BF_[:, 0:T], c(C_BG), sg[0][:], ALU.add, ALU.mult).then_inc(sem("o_taken"), 1)
                    v.wait_ge(sem("l_taken"), j + 2)
                    st(v.tensor_tensor(gt[:], gx[:], gx[:], ALU.mult))
                    st(v.tensor_scalar(gt[:], gt[:], GELU_A, 1.0, ALU.mult, ALU.add))
                    v.tensor_tensor(gt[:], gt[:], gx[:], ALU.mult).then_inc(sem("gelu_arg"), 1)
                    v.wait_ge(pe_sem["sc_done"], j + 1)
                    v.tensor_tensor(sc[:], B4[:, 0:TT * CHUNK].rearrange("p (t c) -> p t c", t=TT),
                                    cmask[:].rearrange("p (a c) -> p a c", a=1).broadcast_to([P, TT, CHUNK]),
                                    ALU.mult).then_inc(sem("sc_ready"), 1)
                    v.wait_ge(pe_sem["kv_done"], j + 1)
                    st(v.tensor_copy(S[:, 0], B7[:, 384:512]))
                    for n in range(1, NCH):
                        ins = v.scalar_tensor_tensor(S[:, n], S[:, n - 1], eb[:, n * CHUNK - 1:n * CHUNK],
                                                     (B5, B6)[(n - 1) % 2][:, (n - 1) // 2 * P:((n - 1) // 2 + 1) * P], ALU.mult, ALU.add)
                        if n < NCH - 1:
                            st(ins)
                        else:
                            ins.then_inc(sem("S_ready"), 1)
                    v.wait_ge(sem("ri_taken"), j + 2)
                    v.wait_ge(sem("a_ready"), j + 1)
                    st.add(v.tensor_tensor(ii[:], ii[:], xc[:], ALU.mult))
                    st(v.tensor_scalar(u[:], pp[:], 1.0, None, ALU.add))
                    st(v.reciprocal(u[:], u[:]))
                    v.tensor_tensor(pp[:], pp[:], u[:], ALU.mult).then_inc(sem("u2_ready"), 1)
                    v.wait_ge(sem("gelu_sig"), j + 1)
                    st(v.tensor_tensor(gx[:], gx[:], gt[:], ALU.mult))
                    v.wait_ge(sem("u_root"), j + 1)
                    st(v.tensor_tensor(u[:], pp[:], ii[:], ALU.mult))
                    st(v.tensor_tensor_scan(pp[:], la[:], u[:], 0.0, ALU.mult, ALU.add))
                    st(v.tensor_tensor(gx[:], gx[:], pp[:, META:TA], ALU.mult))
                    v.wait_ge(sem("lru_taken"), j + 2)
                    st(v.tensor_tensor(gx[:], gx[:], sg[2][:], ALU.mult))
                    v.wait_ge(sem("rms_ready"), j + 1)
                    st(v.reciprocal(y[:], rms[:]))
                    for h, bank in enumerate((B4, B6)):
                        st(v.scalar_tensor_tensor(halves(y)[:, :, h], of_half(bank), c(C_NG), halves(y)[:, :, h],
                                                  ALU.mult, ALU.mult))
                    v.wait_ge(sem("o_taken"), j + 2)
                    st(v.tensor_tensor(y[:], y[:], sg[0][:], ALU.mult))
                    v.wait_ge(sem("hg_taken"), j + 2)
                    st(v.tensor_tensor(y[:], y[:], sg[1][:], ALU.mult))
                    v.tensor_tensor(merged[:, bass.ds(j, 1), :].rearrange("p a t -> p (a t)"), y[:], gx[:],
                                    ALU.add).then_inc(sem("merged_done"), 1)
                    assert st.n == N, st.n
    if stop <= 2:
        dump(nc, sem, dbg, merged[:, :, :])


def load_chunk(sp, a, raw, sem, slot, expert, c):
    src = a["w_gate_up"][expert, :, c] if c < 2 else a["w_down"][expert]
    return sp.dma_start(raw[:, slot], src).then_inc(sem(f"raw_here_{slot}"), 16)


def out_and_route(nc, a, sem, sb, banks, pair, mem, stop, dbg):
    ident, ones, acc, merged, raw = (mem[n] for n in ("ident", "ones", "acc", "merged", "raw"))
    x_hi, x_lo = mem["x_hi"], mem["x_lo"]
    w_out = sb("w_out", [P, HEADS, D])
    g1 = sb("g1", [P, D])
    b1 = sb("b1", [P, D])
    h1T = sb("h1T", [P, KB, T])
    rw = sb("rw", [P, KB, E])
    rbias = sb("rbias", [P, E])
    ws_gu = sb("ws_gu", [P, KB, 2 * F])
    ws_dn = sb("ws_dn", [P, 2, D])
    aT = sb("aT", [P, 2, T])
    stats = sb("stats1", [P, TT, 2, 6])
    mv = sb("mv1", [P, TT, 2])
    rs = sb("rs1", [P, TT, 2])
    before = sb("before", [P, P])
    before2 = sb("before2", [P, P])
    onehot = sb("onehot", [P, ITEMS])
    steps64 = sb("steps64", [P, 12])
    steps4 = sb("steps4", [P, 12])
    e_col = sb("e_col", [P, 1])
    iota = mem["iota"]

    with nc.Block() as block:
        for_out = [sem(f"w_out_here{n}") for n in range(2)]

        @block.sync
        def _(sp):
            for n in range(2):
                sp.dma_start(w_out[:, :, n * 512:(n + 1) * 512], a["w_out"][:, :, n * 512:(n + 1) * 512])\
                  .then_inc(for_out[n], 16)
            sp.dma_start(g1[:], a["norm_rows"][2:3].broadcast_to([P, D])).then_inc(sem("ln1_here"), 16)
            sp.dma_start(b1[:], a["norm_rows"][3:4].broadcast_to([P, D])).then_inc(sem("ln1_here"), 16)
            for t, n in ((rw, "router_w"), (rbias, "router_bias"), (before, "before"), (before2, "before2"),
                         (steps64, "steps64"), (steps4, "steps4"), (e_col, "e_col"), (iota, "iota"),
                         (onehot, "onehot")):
                src = a[n].broadcast_to([P, E]) if n == "router_bias" else a[n]
                sp.dma_start(t[:], src).then_inc(sem("route_here"), 16)
            sp.dma_start(ws_gu[:], a["ws_gate_up"]).then_inc(sem("shared_here"), 16)
            sp.dma_start(ws_dn[:], a["ws_down"]).then_inc(sem("shared_here"), 16)
            for n in range(RAW - 2):
                load_chunk(sp, a, raw, sem, n, n // CHUNKS, n % CHUNKS)

        @block.tensor
        def _(pe):
            for t in range(TT):
                if t >= 2:
                    pe.wait_ge(sem("mix_taken"), t - 1)
                for n in range(2):
                    if t == 0:
                        pe.wait_ge(for_out[n], 16)
                    for j in range(HEADS):
                        last = pe.matmul(banks[2 * (t % 2) + n][:, :], merged[:, j, t * P:(t + 1) * P],
                                         w_out[:, j, n * 512:(n + 1) * 512], start=(j == 0), stop=(j == HEADS - 1))
                last.then_inc(sem("mix_done"), 1)
            for t in range(TT):
                pe.wait_ge(sem("h1_ready"), t + 1)
                if t >= 2:
                    pe.wait_ge(sem("h1T_taken"), t - 1)
                for k in range(KB):
                    last = pe.transpose(pair[2 + t % 2][:, k * P:(k + 1) * P], acc[:, t, k::KB], ident[:])
                last.then_inc(sem("h1T_done"), 1)

        @block.vector
        def _(v):
            st = Steps(v, sem("ln1_step"))
            v.wait_ge(sem("ln1_here"), 32)

            def normed(t):
                v.wait_ge(sem("std1_ready"), t + 1)
                st(v.reciprocal(rs[:, t, 0:1], rs[:, t, 1:2]))
                st(v.tensor_scalar(acc[:, t], acc[:, t], mv[:, t, 0:1], rs[:, t, 0:1], ALU.subtract, ALU.mult))
                st(v.tensor_tensor(acc[:, t], acc[:, t], g1[:], ALU.mult))
                v.tensor_tensor(acc[:, t], acc[:, t], b1[:], ALU.add).then_inc(sem("h1_ready"), 1)

            def part_lo(t):
                v.wait_ge(sem("x_hi_ready"), t + 1)
                v.tensor_tensor(x_lo[:, t], acc[:, t].rearrange("p (q k) -> p k q", k=KB), x_hi[:, t].bitcast(F32),
                                ALU.subtract)

            for t in range(TT):
                v.wait_ge(sem("mix_done"), t + 1)
                v.scalar_tensor_tensor(acc[:, t], acc[:, t], ALPHA, pair[t % 2][:, :], ALU.mult, ALU.add)\
                 .then_inc(sem("mix_taken"), 1)
                v.wait_ge(sem("mix_taken"), t + 1)
                st(v.bn_stats(stats[:, t, 0], acc[:, t, 0:512]))
                st(v.bn_stats(stats[:, t, 1], acc[:, t, 512:1024]))
                st(v.bn_aggr(mv[:, t], stats[:, t]))
                v.tensor_scalar(rs[:, t, 0:1], mv[:, t, 1:2], LN_EPS, None, ALU.add).then_inc(sem("var1_ready"), 1)
                normed(t)
                if t:
                    part_lo(t - 1)
            part_lo(TT - 1)

        @block.scalar
        def _(act):
            for t in range(TT):
                act.wait_ge(sem("var1_ready"), t + 1)
                act.activation(rs[:, t, 1:2], rs[:, t, 0:1], ACT.Sqrt).then_inc(sem("std1_ready"), 1)
                act.wait_ge(sem("h1_ready"), t + 1)
                act.activation(x_hi[:, t], acc[:, t].rearrange("p (q k) -> p k q", k=KB), ACT.Copy)\
                   .then_inc(sem("x_hi_ready"), 1)
                act.wait_ge(sem("h1T_done"), t + 1)
                act.activation(h1T[:, :, t * P:(t + 1) * P], pair[2 + t % 2][:, :].rearrange("p (k c) -> p k c", k=KB),
                               ACT.Copy).then_inc(sem("h1T_taken"), 1)

    sc = sb("scores", [P, TT, E])
    bs = sb("biased", [P, TT, E])
    top8 = sb("top8", [P, TT, 8])
    above = sb("above", [P, TT, E])
    tie = sb("tie", [P, TT, E])
    ties = sb("ties", [P, TT, E])
    room = sb("room", [P, TT])
    chosen = sb("chosen", [P, TT, 2, E])
    norm = sb("norm", [P, TT, 2])
    pw = sb("pw", [P, TT, 2 * E])
    pwT = sb("pwT", [P, TT, P])
    cnt = sb("cnt", [P, 4])
    tmp = sb("tmp", [P, 12])
    d1 = sb("d1", [P, EXTRA])
    d2 = sb("d2", [P, EXTRA])
    base = sb("base", [P, ITEMS])
    left1 = sb("left1", [P, TT, ITEMS])
    left2 = sb("left2", [P, TT, ITEMS])
    q2 = sb("q2", [1, 16])
    with nc.Block() as block:
        R, PO, W_, SM = banks[0], banks[1], banks[6], banks[7]

        @block.sync
        def _(sp):
            for n in range(RAW - 2, RAW):
                load_chunk(sp, a, raw, sem, n, n // CHUNKS, n % CHUNKS)

        @block.tensor
        def _(pe):
            pe.wait_ge(sem("route_here"), 16 * 9)
            for t in range(TT):
                for k in range(KB):
                    last = pe.matmul(R[:, t * E:(t + 1) * E], h1T[:, k, t * P:(t + 1) * P], rw[:, k],
                                     start=(k == 0), stop=(k == KB - 1))
            last.then_inc(sem("logits_done"), 1)
            pe.wait_ge(sem("shared_here"), 32)
            for m in range(4):
                for k in range(KB):
                    last = pe.matmul(banks[2 + m][:, :], ws_gu[:, k, m * P:(m + 1) * P], h1T[:, k],
                                     start=(k == 0), stop=(k == KB - 1))
                last.then_inc(sem("shared_up_done"), 1)
            pe.wait_ge(sem("chosen_ready"), 1)
            for t in range(TT):
                for u in range(t):
                    pe.matmul(PO[:, t * E:(t + 1) * E], ones[:], chosen[:, u, 0], start=(u == 0), stop=False)
                last = pe.matmul(PO[:, t * E:(t + 1) * E], before[:], chosen[:, t, 0], start=(t == 0), stop=True)
            last.then_inc(sem("place_done"), 1)
            for t in range(TT):
                last = pe.matmul(SM[:, 0:1], chosen[:, t].rearrange("p a e -> p (a e)"), ones[:, 0:1],
                                 start=(t == 0), stop=(t == TT - 1))
            last.then_inc(sem("count_done"), 1)
            pe.wait_ge(sem("a_shared_ready"), 2)
            for t in range(TT):
                if t == 1:
                    pe.wait_ge(sem("further_ready"), 1)
                    pe.matmul(SM[:, 1:2], before2[:], cnt[:, 1:2], start=True, stop=True).then_inc(sem("start_done"), 1)
                if t == 2:
                    pe.wait_ge(sem("pw_ready"), 1)
                    for u in range(TT):
                        last = pe.transpose(PO[:, u * P:(u + 1) * P], pw[:, u], ident[:])
                    last.then_inc(sem("pwT_done"), 1)
                if t >= 2:
                    pe.wait_ge(sem("shared_taken"), t - 1)
                for n in range(2):
                    for j in range(2):
                        last = pe.matmul(banks[2 + 2 * (t % 2) + n][:, :], aT[:, j, t * P:(t + 1) * P],
                                         ws_dn[:, j, n * 512:(n + 1) * 512], start=(j == 0), stop=(j == 1))
                last.then_inc(sem("shared_done"), 1)
            pe.wait_ge(sem("items_ready"), 1)
            pe.wait_ge(sem("pwT_ready"), 1)
            for t in range(TT):
                o = R[:, t * ITEMS:(t + 1) * ITEMS]
                pe.matmul(o, pwT[0:E, t], onehot[0:E], start=True, stop=False)
                pe.matmul(o, ones[0:E], base[0:E], start=False, stop=True)
            for t in range(TT):
                pe.matmul(W_[:, t * ITEMS:(t + 1) * ITEMS], pwT[E:P, t], onehot[E:P], start=True, stop=True)
            pe.matmul(SM[0:1, 0:ITEMS], e_col[0:E], onehot[0:E], start=True, stop=True)
            pe.matmul(SM[0:1, ITEMS:ITEMS + 1], ones[0:E, 0:1], cnt[0:E, 1:2], start=True, stop=True)\
              .then_inc(sem("tables_done"), 1)

        @block.scalar
        def _(act):
            act.wait_ge(sem("logits_done"), 1)
            act.activation(sc[:].rearrange("p t e -> p (t e)"), R[:, 0:TT * E], ACT.Sigmoid).then_inc(sem("scores_ready"), 1)
            for j in range(2):
                act.wait_ge(sem("shared_up_done"), j + 1)
                act.activation(aT[:, j], banks[2 + j][:, :], ACT.Silu).then_inc(sem("silu_ready"), 1)
            act.wait_ge(sem("pwT_done"), 1)
            act.activation(pwT[:].rearrange("p t c -> p (t c)"), PO[:, :], ACT.Copy).then_inc(sem("pwT_ready"), 1)

        @block.vector
        def _(v):
            st = Steps(v, sem("route_step"))
            each = lambda x, n=E: x.broadcast_to([P, TT, n])
            v.wait_ge(sem("route_here"), 16 * 9)
            v.wait_ge(sem("scores_ready"), 1)
            st(v.tensor_tensor(bs[:], sc[:], each(rbias[:].rearrange("p (a e) -> p a e", a=1)), ALU.add))
            for t in range(TT):
                st.add(v.max(top8[:, t], bs[:, t]))
            st.sync()
            sixth = top8[:, :, TOP_K - 1:TOP_K]
            st(v.tensor_tensor(above[:], bs[:], each(sixth), ALU.is_gt))
            st(v.tensor_tensor(tie[:], bs[:], each(sixth), ALU.is_equal))
            st(v.tensor_reduce(room[:], above[:], AX, ALU.add))
            st(v.tensor_scalar(room[:], room[:], -1.0, float(TOP_K), ALU.mult, ALU.add))
            for t in range(TT):
                st.add(v.tensor_tensor_scan(ties[:, t], ones[:, 0:E], tie[:, t], 0.0, ALU.mult, ALU.add))
            st.sync()
            st(v.tensor_tensor(ties[:], ties[:], each(room[:].rearrange("p (t a) -> p t a", a=1)), ALU.is_le))
            st(v.tensor_tensor(ties[:], ties[:], tie[:], ALU.mult))
            st(v.tensor_tensor(chosen[:, :, 0], ties[:], above[:], ALU.add))
            v.tensor_copy(chosen[:, :, 1], chosen[:, :, 0]).then_inc(sem("chosen_ready"), 1)
            st(v.tensor_tensor(sc[:], sc[:], chosen[:, :, 0], ALU.mult))
            st(v.tensor_reduce(norm[:, :, 0], sc[:], AX, ALU.add))
            st(v.reciprocal(norm[:, :, 1], norm[:, :, 0]))
            st(v.tensor_scalar(norm[:, :, 1], norm[:, :, 1], ROUTED_SCALE, None, ALU.mult))
            st(v.tensor_tensor(pw[:, :, E:2 * E], sc[:], each(norm[:, :, 1:2]), ALU.mult))
            v.wait_ge(sem("place_done"), 1)
            v.scalar_tensor_tensor(pw[:, :, 0:E], PO[:, 0:TT * E].rearrange("p (t e) -> p t e", t=TT), FAR,
                                   chosen[:, :, 0], ALU.add, ALU.mult).then_inc(sem("pw_ready"), 1)
            v.wait_ge(sem("count_done"), 1)
            st(v.tensor_copy(cnt[:, 0:1], SM[:, 0:1]))
            st(v.tensor_scalar(tmp[:], steps64[:], cnt[:, 0:1], None, ALU.is_lt))
            v.tensor_reduce(cnt[:, 1:2], tmp[:], AX, ALU.add).then_inc(sem("further_ready"), 1)
            for j in range(2):
                v.wait_ge(sem("silu_ready"), j + 1)
                v.wait_ge(sem("shared_up_done"), j + 3)
                v.tensor_tensor(aT[:, j], aT[:, j], banks[4 + j][:, :], ALU.mult).then_inc(sem("a_shared_ready"), 1)
            v.wait_ge(sem("start_done"), 1)
            st(v.tensor_copy(cnt[:, 2:3], SM[:, 1:2]))
            st(v.tensor_scalar(d1[:], iota[:, 0:EXTRA], cnt[:, 2:3], None, ALU.subtract))
            st.add(v.memset(base[:], 0.0))
            st(v.tensor_scalar(d2[:], d1[:], cnt[:, 1:2], None, ALU.is_lt))
            st(v.scalar_tensor_tensor(onehot[:, E:ITEMS], d1[:], 0.0, d2[:], ALU.is_ge, ALU.mult))
            st(v.tensor_scalar(d1[:], d1[:], -float(SLOTS), -float(SLOTS), ALU.mult, ALU.add))
            v.tensor_tensor(base[:, E:ITEMS], d1[:], onehot[:, E:ITEMS], ALU.mult).then_inc(sem("items_ready"), 1)
            for t in range(TT):
                v.wait_ge(sem("shared_done"), t + 1)
                v.scalar_tensor_tensor(acc[:, t], acc[:, t], ALPHA, pair[1 + t % 2][:, :], ALU.mult, ALU.add)\
                 .then_inc(sem("shared_taken"), 1)
            st.add(v.memset(mem["slot_of"][:, ITEMS:], -FAR))
            v.wait_ge(sem("tables_done"), 1)
            st.add(v.tensor_scalar(mem["slot_of"][:, 0:ITEMS].rearrange("p i t -> p t i"),
                                   R[:, 0:TT * ITEMS].rearrange("p (t i) -> p t i", t=TT), FAR, None, ALU.subtract))
            w3 = mem["weight_of"][:].rearrange("p i t n -> p t i n")
            left = [W_[:, 0:TT * ITEMS].rearrange("p (t i) -> p t i", t=TT), left1[:], left2[:]]
            for n in range(3):
                st(v.tensor_copy(w3[:, :, :, n], left[n]))
                if n < 2:
                    st(v.tensor_tensor(left[n + 1], left[n], w3[:, :, :, n], ALU.subtract))
            st.add(v.tensor_copy(mem["expert_of"][:], SM[0:1, 0:ITEMS]))
            st(v.tensor_copy(q2[:, 12:13], SM[0:1, ITEMS:ITEMS + 1]))
            st(v.tensor_scalar(q2[:, 0:12], steps4[0:1], q2[:, 12:13], None, ALU.is_lt))
            st(v.tensor_reduce(q2[:, 13:14], q2[:, 0:12], AX, ALU.add))
            st(v.tensor_scalar(q2[:, 14:15], q2[:, 13:14], float(E // QUAD), None, ALU.add))
            st(v.tensor_copy(mem["quads"][:], q2[:, 14:15]))

    if stop <= 3:
        dump(nc, sem, dbg, acc[:, :, :])


def experts(nc, a, sem, sb, banks, pair, mem, stop, dbg):
    ident, acc, raw, iota = (mem[n] for n in ("ident", "acc", "raw", "iota"))
    x_parts, slot_of, weight_of = (mem["x_hi"], mem["x_lo"]), mem["slot_of"], mem["weight_of"]
    split = [sb(f"split{n}", [P, 2, CHUNK_W], F32R) for n in range(CHUNKS)]
    xg = sb("xg", [P, QUAD, KB, 2, SLOTS], F32R)
    gu = sb("gu", [P, 2 * F])
    act_s = sb("act_s", [P, 2, SLOTS])
    act_a = sb("act_a", [P, 2, SLOTS])
    a_in = sb("a_in", [P, 2, 2, 2, SLOTS], F32R)
    Sr = sb("Sr", [P, TT, QUAD, SLOTS], F32R)
    Sb = sb("Sb", [P, TT, QUAD, 2, SLOTS], BF16)
    ST = [sb(f"ST{n}", [P, TT, P], F32R) for n in range(QUAD)]
    wcol = sb("wcol", [P, QUAD])
    y = [sb(f"y{n}", [P, D], F32R) for n in range(QUAD)]
    two = sb("two", [P, SLOTS])
    ident_b = sb("ident_b", [P, P], BF16)
    GU, TR, XG, WC, SUM, Y = banks[0], banks[1], banks[2:4], banks[6], banks[6:8], (pair[2], pair[3])
    LD = 1408
    flat = lambda x: x.rearrange("p a s -> p (a s)")

    def quads(eng):
        return eng.value_load(mem["quads"][0:1, 0:1], min_val=E // QUAD, max_val=QUADS_MAX)

    with nc.Block() as block:
        @block.sync
        def _(sp):
            sp.dma_start(two[:], a["two"]).then_inc(sem("two_here"), 16)

            def load(i, u, expert):
                for c in range(CHUNKS):
                    sp.wait_ge(sem(f"hi{c}_ready"), i - 1)
                    sp.wait_ge(sem(f"lo{c}_dve"), i - 1)
                    sp.wait_ge(sem(f"lo{c}_pool"), i - 1)
                    sp.wait_ge(sem("two_here"), 16)
                    load_chunk(sp, a, raw, sem, (CHUNKS * u + c) % RAW, expert, c)

            for i in range(2, QUAD):
                load(i, i, i)
            n_quads = quads(sp)
            with sp.Fori(1, n_quads) as q:
                for u in range(QUAD):
                    e = sp.value_load(mem["expert_of"][0:1, bass.ds(QUAD * q + u, 1)], min_val=0, max_val=E - 1)
                    load(QUAD * q + u, u, e)
            for c in range(2):
                sp.wait_ge(sem(f"raw_here_{c}"), 32 * n_quads)
                sp.sem_inc(sem(f"raw_here_{c}"), 16)

        @block.tensor
        def _(pe):
            def split_here(i, c):
                for name in (f"hi{c}_ready", f"lo{c}_dve", f"lo{c}_pool"):
                    pe.wait_ge(sem(name), i + 1)

            def gather(r):
                pe.wait_ge(sem("S_half"), r + 1)
                for k in range(KB):
                    if k >= 2:
                        pe.wait_ge(sem("xg_act" if k % 2 == 0 else "xg_dve"), 4 * r + k // 2)
                    for part in range(2):
                        for t in range(TT):
                            last = pe.matmul(XG[k % 2][:, part * 256:(part + 1) * 256], x_parts[part][:, t, k],
                                             Sr[:, t].rearrange("p u s -> p (u s)"), start=(t == 0), stop=(t == TT - 1))
                    last.then_inc(sem("x_done"), 1)

            def gate_up(i, u):
                for c in range(2):
                    split_here(i, c)
                    for k in range(KB // 2):
                        for part in range(2):
                            last = pe.matmul(GU[:, :], flat(xg[:, u, (KB // 2) * c + k]),
                                             split[c][:, part, k * 2 * F:(k + 1) * 2 * F],
                                             start=(c == 0 and k == 0 and part == 0),
                                             stop=(c == 1 and k == KB // 2 - 1 and part == 1))
                    last.then_inc(sem("gate_up_half"), 1)

            def turn(i):
                pe.wait_ge(sem("gu_ready"), i + 1)
                for m in range(4):
                    last = pe.matmul(TR[:, m * SLOTS:(m + 1) * SLOTS], gu[:, m * P:(m + 1) * P], two[:],
                                     start=True, stop=True)
                last.then_inc(sem("tr_done"), 1)

            def down(i, u):
                pe.wait_ge(sem("a_in_ready"), i + 1)
                split_here(i, 2)
                if u >= 2:
                    pe.wait_ge(sem("y_ready"), i)
                for n in range(2):
                    for j in range(2):
                        for m, (pa, pw) in enumerate(((0, 0), (0, 1), (1, 0))):
                            last = pe.matmul(Y[u % 2][:, n * 512:(n + 1) * 512], flat(a_in[:, j, pa]),
                                             split[2][:, pw, j * D + n * 512:j * D + (n + 1) * 512],
                                             start=(j == 0 and m == 0), stop=(j == 1 and m == 2))
                last.then_inc(sem("y_done"), 1)

            def scatter(q, g0, g1):
                for g in range(g0, g1):
                    t, n = g // 2, g % 2
                    pe.wait_ge(sem("sum_free"), 2 * TT * q + g + 1)
                    for u in range(QUAD):
                        last = pe.matmul(SUM[g % 2][:, :], ST[u][:, t], y[u][:, n * 512:(n + 1) * 512],
                                         start=(u == 0), stop=(u == QUAD - 1))
                    last.then_inc(sem("sum_done"), 1)

            def slots_turned(q):
                pe.wait_ge(sem("S_built"), q + 1)
                pe.wait_ge(sem("sum_free"), 2 * TT * q + 2 * TT + 2)
                for u in range(QUAD):
                    for t in range(TT):
                        at = (u % 2) * 512 + t * P
                        pe.transpose(XG[u // 2].bitcast(BF16)[:, at:at + P], flat(Sb[:, t, u]), ident_b[:])
                        last = pe.matmul(WC[:, (u * TT + t) * 3:(u * TT + t) * 3 + 3], flat(Sb[:, t, u]),
                                         weight_of[:, bass.ds(QUAD * q + u, 1), t], start=True, stop=True)
                last.then_inc(sem("st_done"), 1)

            pe.wait_ge(sem("two_here"), 16)
            for name in ("y_done", "ST_act", "ST_dve"):
                pe.sem_inc(sem(name), 1)
            gather(0)
            n_quads = quads(pe)
            with pe.Fori(0, n_quads) as q:
                i = QUAD * q
                pe.wait_ge(sem("xg_act"), 4 * q + 4)
                pe.wait_ge(sem("xg_dve"), 4 * q + 4)
                gate_up(i, 0)
                pe.wait_ge(sem("y_ready"), QUAD * q + 1)
                pe.wait_ge(sem("ST_act"), q + 1)
                pe.wait_ge(sem("ST_dve"), q + 1)
                scatter(q, 0, 4)
                turn(i)
                scatter(q, 4, 8)
                gate_up(i + 1, 1)
                slots_turned(q)
                down(i, 0)
                turn(i + 1)
                gate_up(i + 2, 2)
                pe.wait_ge(sem("ST_dve"), q + 2)
                down(i + 1, 1)
                turn(i + 2)
                gate_up(i + 3, 3)
                down(i + 2, 2)
                turn(i + 3)
                pe.wait_ge(sem("ST_act"), q + 2)
                gather(q + 1)
                down(i + 3, 3)
            pe.wait_ge(sem("y_ready"), QUAD * n_quads + 1)
            scatter(n_quads, 0, 8)

        def here(eng, q, u, c):
            n = CHUNKS * u + c
            eng.wait_ge(sem(f"raw_here_{n % RAW}"), 16 * (2 * q + n // RAW) + 16)
            return raw[:, n % RAW]

        def xg_out(k):
            return xg[:, :, k].rearrange("p u a s -> p a u s")

        def xg_in(k):
            return XG[k % 2].rearrange("p (a u s) -> p a u s", a=2, u=QUAD)

        @block.scalar
        def _(act):
            def split_hi(q, u, c):
                act.activation(split[c][:, 0], here(act, q, u, c), ACT.Copy).then_inc(sem(f"hi{c}_ready"), 1)

            def y_first(q, i, u):
                act.wait_ge(sem("wcol_ready"), q + 1)
                act.wait_ge(sem("y_done"), i + 2)
                act.activation(y[u][:], Y[u % 2][:, :], ACT.Copy, scale=wcol[:, u:u + 1]).then_inc(sem("y_hi_ready"), 1)

            def take_x(r):
                for k in range(0, KB, 2):
                    act.wait_ge(sem("x_done"), KB * r + k + 1)
                    act.activation(xg_out(k), xg_in(k), ACT.Copy).then_inc(sem("xg_act"), 1)

            for c in range(2):
                split_hi(0, 0, c)
            take_x(0)
            with act.Fori(0, quads(act)) as q:
                for u in range(QUAD):
                    i = QUAD * q + u
                    act.wait_ge(sem("gate_up_half"), 2 * i + 1)
                    split_hi(q, u + 1, 0)
                    act.wait_ge(sem("gate_up_half"), 2 * i + 2)
                    act.activation(gu[:], GU[:, :], ACT.Copy).then_inc(sem("gu_ready"), 1)
                    split_hi(q, u + 1, 1)
                    if u == 1:
                        act.wait_ge(sem("st_done"), q + 1)
                        for m in range(2):
                            ins = act.activation(ST[m][:].rearrange("p t c -> p (t c)"),
                                                 XG[0].bitcast(BF16)[:, m * 512:(m + 1) * 512], ACT.Copy)
                        ins.then_inc(sem("ST_act"), 1)
                    act.wait_ge(sem("y_done"), i + 1)
                    split_hi(q, u, 2)
                    if u:
                        y_first(q, i - 1, u - 1)
                    act.wait_ge(sem("tr_done"), i + 1)
                    act.activation(flat(act_s[:]), TR[:, 0:2 * SLOTS], ACT.Silu).then_inc(sem("silu2_ready"), 1)
                take_x(q + 1)
                y_first(q, QUAD * q + QUAD - 1, QUAD - 1)

        def split_lo(eng, q, u, c, cols, name):
            eng.wait_ge(sem(f"hi{c}_ready"), QUAD * q + u + 1)
            n = CHUNKS * u + c
            eng.tensor_tensor(split[c][:, 1, cols], raw[:, n % RAW, cols], split[c][:, 0, cols].bitcast(F32),
                              ALU.subtract).then_inc(sem(name), 1)

        @block.vector
        def _(v):
            def build(r):
                at = slot_of[:, bass.ds(QUAD * r, QUAD)].rearrange("p u t -> p t u")\
                    .rearrange("p t (u s) -> p t u s", s=1)
                row = iota[:].rearrange("p (t u s) -> p t u s", t=1, u=1)
                v.tensor_tensor(Sr[:], row.broadcast_to([P, TT, QUAD, SLOTS]), at.broadcast_to([P, TT, QUAD, SLOTS]),
                                ALU.is_equal).then_inc(sem("S_half"), 1)

            def lo(q, u, c):
                split_lo(v, q, u, c, slice(0, LD), f"lo{c}_dve")

            def take_x(r):
                for k in range(1, KB, 2):
                    v.wait_ge(sem("x_done"), KB * r + k + 1)
                    v.tensor_copy(xg_out(k), xg_in(k)).then_inc(sem("xg_dve"), 1)

            def y_second(i, u):
                v.wait_ge(sem("y_hi_ready"), i + 1)
                v.scalar_tensor_tensor(y[u][SLOTS:P], Y[u % 2][SLOTS:P, :], wcol[SLOTS:P, u:u + 1],
                                       y[u][SLOTS:P].bitcast(F32), ALU.mult, ALU.subtract).then_inc(sem("y_ready"), 1)

            def add_up(q, g0, g1):
                for g in range(g0, g1):
                    v.wait_ge(sem("sum_done"), 2 * TT * q + g + 1)
                    part = acc[:, g // 2, (g % 2) * 512:(g % 2 + 1) * 512]
                    v.tensor_tensor(part, part, SUM[g % 2][:, :], ALU.add).then_inc(sem("sum_free"), 1)

            build(0)
            v.tensor_copy(ident_b[:], ident[:])
            v.sem_inc(sem("sum_free"), 2)
            for c in range(2):
                lo(0, 0, c)
            take_x(0)
            n_quads = quads(v)
            with v.Fori(0, n_quads) as q:
                for u in range(QUAD):
                    i = QUAD * q + u
                    lo(q, u + 1, 0)
                    if u == 0:
                        add_up(q, 0, 4)
                    lo(q, u + 1, 1)
                    if u == 0:
                        add_up(q, 4, 8)
                    if u == 1:
                        v.wait_ge(sem("st_done"), q + 1)
                        v.tensor_reduce(wcol[:], WC[:, 0:QUAD * TT * 3].rearrange("p (u n) -> p u n", u=QUAD), AX,
                                        ALU.add).then_inc(sem("wcol_ready"), 1)
                        for m in range(2):
                            ins = v.tensor_copy(ST[2 + m][:].rearrange("p t c -> p (t c)"),
                                                XG[1].bitcast(BF16)[:, m * 512:(m + 1) * 512])
                        ins.then_inc(sem("ST_dve"), 1)
                        build(q + 1)
                    lo(q, u, 2)
                    v.wait_ge(sem("silu2_ready"), i + 1)
                    v.tensor_tensor(flat(act_a[:]), flat(act_s[:]), TR[:, 2 * SLOTS:4 * SLOTS], ALU.mult)\
                     .then_inc(sem("aa_ready"), 1)
                    v.wait_ge(sem("aa_ready"), i + 1)
                    twice = act_a[:].rearrange("p j (a s) -> p j a s", a=1).broadcast_to([P, 2, 2, SLOTS])
                    v.tensor_copy(a_in[:, :, 0], twice).then_inc(sem("a_hi_ready"), 1)
                    v.wait_ge(sem("a_hi_ready"), i + 1)
                    v.tensor_tensor(a_in[:, :, 1], twice, a_in[:, :, 0].bitcast(F32), ALU.subtract)\
                     .then_inc(sem("a_in_ready"), 1)
                    if u:
                        y_second(i - 1, u - 1)
                take_x(q + 1)
                y_second(QUAD * q + QUAD - 1, QUAD - 1)
            add_up(n_quads, 0, 8)

        @block.gpsimd
        def _(pool):
            def lo(q, u, c):
                split_lo(pool, q, u, c, slice(LD, CHUNK_W), f"lo{c}_pool")

            def copies(r):
                for m in range(2):
                    ins = pool.tensor_copy(Sb[:, :, :, m], Sr[:].bitcast(F32))
                ins.then_inc(sem("S_built"), 1)

            pool.wait_ge(sem("S_half"), 1)
            copies(0)
            for c in range(2):
                lo(0, 0, c)
            for n in range(QUAD):
                pool.memset(y[n][:].bitcast(F32), 0.0)
                ins = pool.memset(ST[n][:].bitcast(F32), 0.0)
            ins.then_inc(sem("y_ready"), 1)
            with pool.Fori(0, quads(pool)) as q:
                for u in range(QUAD):
                    lo(q, u + 1, 0)
                    lo(q, u + 1, 1)
                    if u == 2:
                        pool.wait_ge(sem("S_half"), q + 2)
                        pool.wait_ge(sem("st_done"), q + 1)
                    lo(q, u, 2)
                    if u == 2:
                        copies(q + 1)


def output_norm(nc, a, sem, sb, mem, out):
    acc = mem["acc"]
    g2 = sb("g2", [P, D])
    b2 = sb("b2", [P, D])
    stats = sb("stats2", [P, TT, 2, 6])
    mv = sb("mv2", [P, TT, 2])
    rs = sb("rs2", [P, TT, 2])
    with nc.Block() as block:
        @block.sync
        def _(sp):
            sp.dma_start(g2[:], a["norm_rows"][4:5].broadcast_to([P, D])).then_inc(sem("ln2_here"), 16)
            sp.dma_start(b2[:], a["norm_rows"][5:6].broadcast_to([P, D])).then_inc(sem("ln2_here"), 16)
            for t in range(TT):
                sp.wait_ge(sem("out_ready"), t + 1)
                sp.dma_start(out[t * P:(t + 1) * P], acc[:, t]).then_inc(sem("stored"), 16)
            sp.wait_ge(sem("stored"), 16 * TT)

        @block.scalar
        def _(act):
            for t in range(TT):
                act.wait_ge(sem("var2_ready"), t + 1)
                act.activation(rs[:, t, 1:2], rs[:, t, 0:1], ACT.Sqrt).then_inc(sem("std2_ready"), 1)

        @block.vector
        def _(v):
            st = Steps(v, sem("ln2_step"))

            def stats_of(t):
                st(v.bn_stats(stats[:, t, 0], acc[:, t, 0:512]))
                st(v.bn_stats(stats[:, t, 1], acc[:, t, 512:1024]))
                st(v.bn_aggr(mv[:, t], stats[:, t]))
                v.tensor_scalar(rs[:, t, 0:1], mv[:, t, 1:2], LN_EPS, None, ALU.add).then_inc(sem("var2_ready"), 1)

            stats_of(0)
            for t in range(TT):
                if t + 1 < TT:
                    stats_of(t + 1)
                v.wait_ge(sem("std2_ready"), t + 1)
                st(v.reciprocal(rs[:, t, 0:1], rs[:, t, 1:2]))
                st(v.tensor_scalar(acc[:, t], acc[:, t], mv[:, t, 0:1], rs[:, t, 0:1], ALU.subtract, ALU.mult))
                v.wait_ge(sem("ln2_here"), 32)
                st(v.tensor_tensor(acc[:, t], acc[:, t], g2[:], ALU.mult))
                v.tensor_tensor(acc[:, t], acc[:, t], b2[:], ALU.add).then_inc(sem("out_ready"), 1)


def dump(nc, sem, dbg, ap):
    with nc.Block() as block:
        @block.sync
        def _(sp):
            sp.dma_start(dbg, ap).then_inc(sem("dumped"), 16)
            sp.wait_ge(sem("dumped"), 16)


def layout(i):
    w = {}
    w["x"] = i["x"][0]
    w["meta"] = i["meta_tokens"]
    w["w_in"] = i["w_in"][0].reshape(P, KB, GROUPS, HEADS, P).transpose(3, 0, 2, 1, 4)[:, :, list(W_ORDER)]
    b = i["b_in"][0].reshape(GROUPS, HEADS, P)
    lb = i["hg_lb_logits"].reshape(2, HEADS, P)
    ng = np.broadcast_to(i["hg_norm_g"].reshape(1, P), (HEADS, P))
    cw = i["conv_w"][0].reshape(CONV_W, HEADS, P)
    h = lambda n: i[n][0].reshape(HEADS, P)
    w["head_cols"] = np.stack([b[GQ], b[GF], b[GO], b[GX], b[GL], b[GHG], b[GLRU], ng, cw[0], cw[1],
                               cw[2], cw[3], h("conv_b"), h("lru_ba"), h("lru_bx")], axis=2)
    w["all_cols"] = np.stack([h("lru_lambda"), lb[0], lb[1]], axis=0).transpose(2, 0, 1)
    w["v_bias"] = b[GV].reshape(HEADS, 1, P)
    w["lru_w"] = np.stack([i["lru_wa"][0], i["lru_wx"][0]], axis=2)
    w["norm_cols"] = np.stack([i["ln_in_g"].reshape(P, KB), i["ln_in_b"].reshape(P, KB)], axis=1)
    w["norm_rows"] = np.stack([i["ln_in_g"], i["ln_in_b"], i["ln1_g"][0], i["ln1_b"][0], i["ln2_g"][0], i["ln2_b"][0]])
    w["ident"] = np.eye(P, dtype=np.float32)
    s, t = np.arange(P)[:, None] % CHUNK, np.arange(CHUNK)[None]
    w["cmask"] = (s <= t).astype(np.float32)
    r = np.ones((P, TA), np.float32)
    r[:, 0] = 0
    r[:, META::CHUNK] = 0
    w["reset"] = r
    w["w_out"] = i["w_out"][0].reshape(HEADS, P, D).transpose(1, 0, 2)
    w["router_w"] = i["router_w"][0].reshape(P, KB, E)
    w["router_bias"] = i["router_bias"]
    w["ws_gate_up"] = np.concatenate([i["ws_gate"][0], i["ws_up"][0]], axis=1).reshape(P, KB, 2 * F)
    w["ws_down"] = i["ws_down"][0].reshape(2, P, D).transpose(1, 0, 2)
    w["w_gate_up"] = np.concatenate([i["we_gate"][0], i["we_up"][0]], axis=2).reshape(E, P, 2, CHUNK_W)
    w["w_down"] = i["we_down"][0].reshape(E, 2, P, D).transpose(0, 2, 1, 3).reshape(E, P, CHUNK_W)
    n = np.arange(P)
    w["before"] = (n[:, None] < n[None]).astype(np.float32)
    w["before2"] = w["before"] * (n[:, None] // E == n[None] // E).astype(np.float32)
    w["onehot"] = np.concatenate([np.tile(np.eye(E, dtype=np.float32), (2, 1)), np.zeros((P, EXTRA), np.float32)], axis=1)
    w["two"] = np.tile(np.eye(SLOTS, dtype=np.float32), (2, 1))
    w["iota"] = np.broadcast_to(np.arange(SLOTS, dtype=np.float32), (P, SLOTS))
    w["e_col"] = (n % E).astype(np.float32).reshape(P, 1)
    w["steps64"] = np.broadcast_to(np.arange(1, 13, dtype=np.float32) * SLOTS, (P, 12))
    w["steps4"] = np.broadcast_to(np.arange(12, dtype=np.float32) * QUAD, (P, 12))
    return {k: np.ascontiguousarray(v) for k, v in w.items()}


def kernel(**inputs):
    import concourse.bacc as bacc
    from concourse.bass_utils import run_bass_kernel_spmd

    arrays = {f"in_{n}": v for n, v in layout({n: np.asarray(v) for n, v in inputs.items()}).items()}
    nc = bacc.Bacc("TRN2", target_bir_lowering=False, num_devices=1)
    aps = {n[3:]: nc.dram_tensor(n, v.shape, mybir.dt.from_np(v.dtype), kind="ExternalInput").ap()
           for n, v in arrays.items()}
    out = nc.dram_tensor("out", (T, D), F32, kind="ExternalOutput").ap()
    program(nc, aps, out)
    result = run_bass_kernel_spmd(nc, [arrays], core_ids=[0])
    return result.results[0]["out"].reshape(1, T, D)
```

```python
from contextlib import ExitStack

import numpy as np
import concourse.bass as bass
from concourse import mybir

P = 128
D = 1024
KB = D // P
META = 16
T = 512
TA = META + T
TT = T // P
HEADS = 8
GROUPS = 8
GQ, GF, GV, GO, GX, GL, GHG, GLRU = range(8)
PAIRS = GROUPS // 2
PARTS = 4
W_ORDER = (GF, GV, GQ, GX, GO, GL, GHG, GLRU)
EARLY = 2
CHUNK = 64
SUB = 16
NSUB = CHUNK // SUB
NCH = T // CHUNK
CONV_W = 4
E = 64
TOP_K = 6
F = 256
SLOTS = 64
EXTRA = T * TOP_K // SLOTS
ITEMS = E + EXTRA
QUAD = 4
QUADS_MAX = ITEMS // QUAD
CHUNK_W = 2048
CHUNKS = 3
RAW = 6
FAR = 4096.0
ALPHA = 2.0 ** 0.25
LN_EPS, RMS_EPS = 1e-5, 1e-6
ROUTED_SCALE = 2.5
GELU_A, GELU_B = 0.044715, 2.0 * 0.7978845608028654
(C_BQ, C_BF, C_BV, C_BG, C_BX, C_BL, C_BHG, C_BLRU, C_NG, C_W0, C_W1, C_W2, C_W3, C_CB, C_BA,
 C_BI) = range(16)
NCOL = 16

ALU = mybir.AluOpType
ACT = mybir.ActivationFunctionType
F32 = mybir.dt.float32
F32R = mybir.dt.float32r
BF16 = mybir.dt.bfloat16
I32 = mybir.dt.int32
AX = mybir.AxisListType.X


class Steps:

    def __init__(self, eng, sem, base=0):
        self.eng, self.sem, self.base, self.n = eng, sem, base, 0

    def __call__(self, ins):
        self.n += 1
        ins.then_inc(self.sem, 1)
        self.eng.wait_ge(self.sem, self.base + self.n)

    def add(self, ins):
        self.n += 1
        ins.then_inc(self.sem, 1)

    def sync(self):
        self.eng.wait_ge(self.sem, self.base + self.n)


def program(nc, a, out, stop=9, dbg=None):
    with ExitStack() as whole:
        sems = {}

        def sem(name):
            if name not in sems:
                sems[name] = whole.enter_context(nc.semaphore(name))
            return sems[name]

        top = [(nc.sbuf_base + 63) // 64 * 64]

        def sb(name, shape, dt=F32, at=None):
            size = int(np.prod(shape[1:])) * (2 if dt == BF16 else 4)
            if at is None:
                at = top[0]
                top[0] += (size + 63) // 64 * 64
                assert top[0] <= nc.sbuf_usable_end, (name, top[0])
            return nc.alloc_sbuf_tensor_at(name, shape, dt, offset=at)

        pair = [whole.enter_context(nc.psum_tensor(f"pair{i}", [P, 1024], F32)) for i in range(4)]
        banks = [pair[i // 2][:, (i % 2) * 512:(i % 2) * 512 + 512] for i in range(8)]

        mem = {}
        mem["ident"] = sb("ident", [P, P])
        mem["ones"] = sb("ones", [P, P])
        mem["acc"] = sb("acc", [P, TT, D])
        raw_at = top[0]
        mem["raw"] = sb("raw", [P, RAW, CHUNK_W])
        mem["merged"] = sb("merged", [P, HEADS, T], at=raw_at + (RAW - 2) * CHUNK_W * 4)
        persist = top[0]
        mem["x_hi"] = sb("x_hi", [P, TT, KB, P], F32R)
        mem["x_lo"] = sb("x_lo", [P, TT, KB, P], F32R)
        mem["slot_of"] = sb("slot_of", [P, ITEMS + QUAD, TT])
        mem["weight_of"] = sb("weight_of", [P, ITEMS, TT, 3], BF16)
        mem["expert_of"] = sb("expert_of", [1, ITEMS], I32)
        mem["quads"] = sb("quads", [1, 1], I32)
        mem["iota"] = sb("iota", [P, SLOTS])
        phase = top[0]
        mem["w_raw"] = sb("w_raw", [P, PAIRS, 2, D])
        after_w = top[0]
        front(nc, a, sem, sb, banks, mem, stop, dbg, top, raw_at, persist, phase, after_w)
        if stop <= 2:
            return
        top[0] = after_w
        out_and_route(nc, a, sem, sb, banks, pair, mem, stop, dbg)
        if stop <= 3:
            return
        top[0] = phase
        experts(nc, a, sem, sb, banks, pair, mem, stop, dbg)
        if stop <= 4:
            dump(nc, sem, dbg, mem["acc"][:, :, :])
            return
        top[0] = phase
        output_norm(nc, a, sem, sb, mem, out)


def project_out(pe, mem, banks, t, n, j):
    return pe.matmul(banks[2 * (t % 2) + n][:, :], mem["merged"][:, j, t * P:(t + 1) * P],
                     mem["w_raw"][:, j // 2, j % 2, n * 512:(n + 1) * 512], start=(j == 0), stop=(j == HEADS - 1))


def front(nc, a, sem, sb, banks, mem, stop, dbg, top, raw_at, persist, phase, after_w):
    ident, ones, acc, merged, w_raw = (mem[n] for n in ("ident", "ones", "acc", "merged", "w_raw"))
    low, low_end = [raw_at], raw_at + (RAW - 2) * CHUNK_W * 4

    def sb_low(name, shape):
        at = low[0]
        low[0] += int(np.prod(shape[1:])) * 4
        assert low[0] <= low_end
        return sb(name, shape, at=at)

    top[0] = persist
    hT = [sb(f"hT{n}", [P, KB, T], F32R) for n in range(2)]
    hTm = sb("hTm", [P, KB, META])
    par = [sb(f"par{s}", [P, NCOL]) for s in range(2)]
    lw = [sb(f"lw{s}", [P, 2, P]) for s in range(2)]
    cols = sb("cols", [P, 2, KB])
    cmask = sb("cmask", [P, CHUNK])
    assert top[0] <= phase
    top[0] = after_w
    w = sb("w_parts", [P, PARTS, 2, D], F32R)
    reset = sb("reset", [P, TA])
    g_row = sb("g_row", [P, D], at=low_end + 4 * T * 4)
    b_row = sb("b_row", [P, D], at=low_end + 6 * T * 4)

    def load_params(sp, j, s):
        sp.dma_start(par[s][:], a["head_cols"][j]).then_inc(sem(f"par_here_{s}"), 16)
        sp.dma_start(lw[s][:], a["lru_w"][j]).then_inc(sem(f"lw_here_{s}"), 16)

    def load_pair(sp, j, m):
        sp.dma_start(w_raw[:, m], a["w_in"][j, :, m]).then_inc(sem(f"w_here_{m}"), 16)

    def split_hi(act, j, n):
        act.wait_ge(sem(f"w_here_{n // 2}"), 16 * j + 16)
        act.activation(w[:, n % PARTS, 0], w_raw[:, n // 2, n % 2], ACT.Copy).then_inc(sem("w_hi_ready"), 1)

    def split_lo(pool, j, n):
        pool.wait_ge(sem("w_hi_ready"), GROUPS * j + n + 1)
        pool.tensor_tensor(w[:, n % PARTS, 1], w_raw[:, n // 2, n % 2], w[:, n % PARTS, 0].bitcast(F32),
                           ALU.subtract).then_inc(sem("w_lo_ready"), 1)

    def residual(eng, st, t):
        st(eng.tensor_tensor(acc[:, t], acc[:, t], g_row[:], ALU.mult))
        st(eng.tensor_tensor(acc[:, t], acc[:, t], b_row[:], ALU.add))

    both = top[0]
    with nc.Block() as block:
        xin = sb("xin", [P, TT + 1, D])
        stats = sb("stats", [P, TT + 1, 2, 6])
        mv = sb("mv", [P, TT + 1, 2])
        rs = sb("rs", [P, TT + 1, 2])
        h = [sb_low(f"h{n}", [P, T]) for n in range(4)]
        x_here = [sem(f"x_here{t}") for t in range(TT + 1)]
        consts, rows_here = sem("consts_here"), sem("rows_here")
        var_ready, std_ready, xn_ready = sem("var_ready"), sem("std_ready"), sem("xn_ready")
        tr_ready = sem("tr_ready")

        @block.sync
        def _(sp):
            for t in range(TT):
                sp.dma_start(xin[:, t], a["x"][t * P:(t + 1) * P]).then_inc(x_here[t], 16)
            sp.dma_start(xin[0:META, TT], a["meta"]).then_inc(x_here[TT], 16)
            sp.dma_start(ident[:], a["ident"]).then_inc(consts, 16)
            sp.dma_start(cols[:, 0:2], a["norm_cols"]).then_inc(consts, 16)
            sp.dma_start(cmask[:], a["cmask"]).then_inc(consts, 16)
            sp.dma_start(reset[:], a["reset"]).then_inc(consts, 16)
            load_pair(sp, 0, 0)
            load_params(sp, 0, 0)
            for m in range(1, PAIRS):
                load_pair(sp, 0, m)
            sp.dma_start(g_row[:], a["norm_rows"][0:1].broadcast_to([P, D])).then_inc(rows_here, 16)
            sp.dma_start(b_row[:], a["norm_rows"][1:2].broadcast_to([P, D])).then_inc(rows_here, 16)

        @block.vector
        def _(v):
            st = Steps(v, sem("dve_step"))
            st.add(v.memset(ones[:], 1.0))
            for t in range(TT + 1):
                n = P if t < TT else META
                v.wait_ge(x_here[t], 16)
                st.add(v.bn_stats(stats[0:n, t, 0], xin[0:n, t, 0:512]))
                st(v.bn_stats(stats[0:n, t, 1], xin[0:n, t, 512:1024]))
                st(v.bn_aggr(mv[0:n, t], stats[0:n, t]))
                v.tensor_scalar(rs[0:n, t, 0:1], mv[0:n, t, 1:2], LN_EPS, None, ALU.add).then_inc(var_ready, 1)
            for t in range(TT + 1):
                n = P if t < TT else META
                v.wait_ge(std_ready, t + 1)
                st(v.reciprocal(rs[0:n, t, 0:1], rs[0:n, t, 1:2]))
                v.tensor_scalar(acc[:, t] if t < TT else xin[0:n, t], xin[0:n, t], mv[0:n, t, 0:1], rs[0:n, t, 0:1],
                                ALU.subtract, ALU.mult).then_inc(xn_ready, 1)
            v.wait_ge(consts, 64)
            for k in range(KB):
                v.wait_ge(sem("h_ready"), k + 1)
                st(v.tensor_copy(hT[0][:, k], h[k % 4][:]))
                v.tensor_tensor(hT[1][:, k], h[k % 4][:], hT[0][:, k].bitcast(F32), ALU.subtract)\
                 .then_inc(sem("h_split"), 1)
            v.wait_ge(tr_ready, KB + 1)
            for k in range(KB):
                v.tensor_scalar(hTm[:, k], banks[4][:, k * META:(k + 1) * META], cols[:, 0, k:k + 1],
                                cols[:, 1, k:k + 1], ALU.mult, ALU.add)

        @block.scalar
        def _(act):
            for t in range(TT + 1):
                n = P if t < TT else META
                act.wait_ge(var_ready, t + 1)
                act.activation(rs[0:n, t, 1:2], rs[0:n, t, 0:1], ACT.Sqrt).then_inc(std_ready, 1)
            act.wait_ge(consts, 64)
            for k in range(KB):
                act.wait_ge(tr_ready, k + 1)
                if k >= 4:
                    act.wait_ge(sem("h_split"), k - 3)
                act.activation(h[k % 4][:], banks[k % 4][:, 0:T], ACT.Identity, scale=cols[:, 0, k:k + 1],
                               bias=cols[:, 1, k:k + 1]).then_inc(sem("h_ready"), 1)
                if k % 2:
                    split_hi(act, 0, k // 2)

        @block.tensor
        def _(pe):
            pe.wait_ge(consts, 64)
            pe.wait_ge(xn_ready, TT + 1)
            for k in range(KB):
                if k >= 4:
                    pe.wait_ge(sem("h_ready"), k - 3)
                for t in range(TT):
                    last = pe.transpose(banks[k % 4][:, t * P:(t + 1) * P], acc[:, t, k::KB], ident[:])
                last.then_inc(tr_ready, 1)
            for k in range(KB):
                last = pe.transpose(banks[4][:, k * META:(k + 1) * META], xin[0:META, TT, k::KB],
                                    ident[0:META, 0:META])
            last.then_inc(tr_ready, 1)

        @block.gpsimd
        def _(pool):
            for n in range(PARTS):
                split_lo(pool, 0, n)

    if stop <= 1:
        dump(nc, sem, dbg, acc[:, :, :])
        return

    top[0] = both
    low[0] = raw_at
    with nc.Block() as block:
        all_cols = sb("all_cols", [P, 3, HEADS])
        lam = sb("lam", [P, 6, HEADS])
        derived = sb("derived", [P, HEADS, 4])
        own = [sb(f"own{s}", [P, 4]) for s in range(2)]
        sig_f = sb_low("sig_f", [P, TA])
        f = sb_low("f", [P, TA])
        kk = sb_low("kk", [P, TA])
        b = sb_low("b", [P, TA])
        q = sb_low("q", [P, T])
        eq = sb_low("eq", [P, T])
        eb = sb_low("eb", [P, T])
        q_in = sb_low("q_in", [P, T])
        q_st = sb_low("q_st", [P, T])
        k_in = sb_low("k_in", [P, NSUB, NCH, CHUNK])
        k_st = sb("k_st", [P, TA])
        kT = sb("kT", [P, TT, P])
        kTm = sb("kTm", [META, P])
        vt = sb("vt", [P, TT, P])
        vm = sb("vm", [META, P])
        sc = sb("sc", [P, TT, CHUNK])
        S = sb_low("S", [P, NCH, P])
        o2 = sb("o2", [P, T])
        vT = o2
        vTm = sb("vTm", [P, META])
        rms = sb("rms", [P, T])
        y = sb("y", [P, T])
        xr = sb("xr", [P, CONV_W - 1 + TA])
        xc = sb("xc", [P, TA])
        rr = sb("rr", [P, TA])
        ii = sb("ii", [P, TA])
        la = sb("la", [P, TA])
        pp = sb("pp", [P, TA])
        u = sb("u", [P, TA])
        gx = sb("gx", [P, T])
        gt = sb("gt", [P, T])
        sg = [sb(f"sg{i}", [P, T]) for i in range(3)]
        eps = sb("eps", [P, 1])

        BF_, BQ_, BV_, BX_ = banks[0], banks[1], banks[2], banks[3]
        B4, B7 = banks[6], banks[7]
        B5, B6 = banks[4], banks[5]
        halves = lambda t: t[:, :].rearrange("p (t h s) -> p t h s", t=TT, h=2)
        of_half = lambda bank: bank[:, 0:TT * CHUNK].rearrange("p (t s) -> p t s", t=TT)
        chunked = lambda t: t.rearrange("p (c s) -> p c s", c=NCH)

        per_head = ("f_done q_done v_done vt_done x_done o_done l_done hg_done lru_done kt_done ri_done sc_done "
                    "kv_done out_done rms_done").split()
        pe_sem = {n: sem("pe_" + n) for n in per_head}

        @block.sync
        def _(sp):
            sp.dma_start(all_cols[:], a["all_cols"]).then_inc(sem("all_cols_here"), 16)

            def load_head(j, s, params=True):
                for m in range(PAIRS):
                    if m < 2:
                        sp.wait_ge(sem("w_lo_ready"), GROUPS * (j - 1) + 6 + 2 * m)
                        sp.wait_ge(sem("all_cols_here"), 16)
                    load_pair(sp, j, m)
                    if m == 0 and params:
                        load_params(sp, j, s)

            load_head(1, 1)
            with sp.Fori(1, HEADS // 2) as r:
                for s in range(2):
                    load_head(2 * r + s, s)
            load_head(HEADS, 0, False)

        @block.tensor
        def _(pe):
            for name in ("o_taken", "ri_taken", "l_taken", "hg_taken", "lru_taken"):
                pe.sem_inc(sem(name), 1)
            with pe.Fori(0, HEADS // 2) as r:
                for s in range(2):
                    j = 2 * r + s

                    def project(bank, g, meta_at=None, after=None):
                        n = W_ORDER.index(g)
                        pe.wait_ge(sem("w_lo_ready"), GROUPS * j + n + 1)
                        for k in range(KB):
                            for m, (pw, ph) in enumerate(((0, 0), (0, 1), (1, 0))):
                                last = pe.matmul(bank[:, 0:T], w[:, n % PARTS, pw, k * P:(k + 1) * P], hT[ph][:, k],
                                                 start=(k == 0 and m == 0), stop=(k == KB - 1 and m == 2))
                        if meta_at is not None:
                            if after:
                                pe.wait_ge(sem(after), j + 1)
                            for k in range(KB):
                                last = pe.matmul(B7[:, meta_at:meta_at + META], w_raw[:, n // 2, n % 2, k * P:(k + 1) * P],
                                                 hTm[:, k], start=(k == 0), stop=(k == KB - 1))
                        return last

                    pe.wait_ge(sem("o_taken"), j + 1)
                    pe.wait_ge(sem("ri_taken"), j + 1)
                    project(BF_, GF, 0).then_inc(pe_sem["f_done"], 1)
                    pe.wait_ge(sem("hg_taken"), j + 1)
                    project(BV_, GV, 64, "f_taken").then_inc(pe_sem["v_done"], 1)
                    pe.wait_ge(sem("l_taken"), j + 1)
                    project(BQ_, GQ).then_inc(pe_sem["q_done"], 1)
                    pe.wait_ge(sem("v_taken"), j + 1)
                    for t in range(TT):
                        pe.transpose(BV_[:, t * P:(t + 1) * P], vT[:, t * P:(t + 1) * P], ident[:])
                    pe.transpose(B7[0:META, 128:256], vTm[:], ident[:]).then_inc(pe_sem["vt_done"], 1)
                    pe.wait_ge(sem("lru_taken"), j + 1)
                    project(BX_, GX, 16, "vt_taken").then_inc(pe_sem["x_done"], 1)
                    pe.wait_ge(sem("f_taken"), j + 1)
                    project(BF_, GO).then_inc(pe_sem["o_done"], 1)

                    pe.wait_ge(sem("qk_ready"), j + 1)
                    for t in range(TT):
                        pe.transpose(B4[:, t * P:(t + 1) * P], k_st[:, META + t * P:META + (t + 1) * P], ident[:])
                    pe.wait_ge(sem("x_taken"), j + 1)
                    pe.transpose(B7[0:META, 256:384], k_st[:, 0:META], ident[:]).then_inc(pe_sem["kt_done"], 1)
                    pe.wait_ge(sem("q_taken"), j + 1)
                    project(BQ_, GL).then_inc(pe_sem["l_done"], 1)

                    pe.wait_ge(sem("xc_ready"), j + 1)
                    pe.wait_ge(sem(f"lw_here_{s}"), 16 * r + 16)
                    pe.wait_ge(sem("kt_taken"), j + 1)
                    for i, bank in enumerate((B5, B6)):
                        pe.matmul(bank[:, 0:T], lw[s][:, i], xc[:, META:TA], start=True, stop=True)
                        last = pe.matmul(B7[:, 32 + 16 * i:48 + 16 * i], lw[s][:, i], xc[:, 0:META],
                                         start=True, stop=True)
                    last.then_inc(pe_sem["ri_done"], 1)

                    pe.wait_ge(sem("kt_taken"), j + 1)
                    for c in range(NCH):
                        t, h0 = c // 2, CHUNK * (c % 2)
                        for i in range(NSUB):
                            last = pe.matmul(B4[h0:h0 + CHUNK, t * CHUNK + i * SUB:t * CHUNK + (i + 1) * SUB],
                                             k_in[:, i, c], q_in[:, c * CHUNK + i * SUB:c * CHUNK + (i + 1) * SUB],
                                             start=True, stop=True)
                    last.then_inc(pe_sem["sc_done"], 1)
                    pe.wait_ge(sem("ri_taken"), j + 2)
                    pe.matmul(B7[:, 384:512], kTm[:], vm[:], start=True, stop=True)
                    for c in range(NCH - 1):
                        t, h0 = c // 2, CHUNK * (c % 2)
                        last = pe.matmul((B5, B6)[c % 2][:, t * P:(t + 1) * P], kT[h0:h0 + CHUNK, t],
                                         vt[h0:h0 + CHUNK, t], start=True, stop=True)
                    last.then_inc(pe_sem["kv_done"], 1)
                    pe.wait_ge(sem("vt_taken"), j + 1)
                    project(BV_, GHG).then_inc(pe_sem["hg_done"], 1)

                    pe.wait_ge(sem("sc_ready"), j + 1)
                    pe.wait_ge(sem("S_ready"), j + 1)
                    for c in range(NCH):
                        t, h0 = c // 2, CHUNK * (c % 2)
                        o = (B4, B6)[c % 2][:, t * CHUNK:(t + 1) * CHUNK]
                        pe.matmul(o, vt[h0:h0 + CHUNK, t], sc[h0:h0 + CHUNK, t], start=True, stop=False)
                        last = pe.matmul(o, S[:, c], q_st[:, c * CHUNK:(c + 1) * CHUNK], start=False, stop=True)
                    last.then_inc(pe_sem["out_done"], 1)
                    pe.wait_ge(sem("x_taken"), j + 1)
                    project(BX_, GLRU).then_inc(pe_sem["lru_done"], 1)
                    pe.wait_ge(sem("o2_ready"), j + 1)
                    pe.matmul(B5[:, 0:T], ones[:], o2[:], start=True, stop=True).then_inc(pe_sem["rms_done"], 1)

            for name in ("o_taken", "l_taken", "hg_taken", "lru_taken"):
                pe.wait_ge(sem(name), HEADS + 1)
            for j in range(HEADS):
                if j % 2 == 0:
                    pe.wait_ge(sem(f"w_here_{j // 2}"), 16 * (HEADS + 1))
                if j == HEADS - 1:
                    pe.wait_ge(sem("merged_done"), HEADS)
                for t in range(EARLY):
                    for n in range(2):
                        last = project_out(pe, mem, banks, t, n, j)
            last.then_inc(sem("mix_done"), EARLY)

        @block.scalar
        def _(act):
            act.wait_ge(sem("eps_ready"), 1)
            act.wait_ge(sem("lam_ready"), 1)
            act.activation(lam[:, 1], lam[:, 0], ACT.Exp)
            act.activation(derived[:, :, 0], derived[:, :, 1], ACT.Sigmoid).then_inc(sem("elam_ready"), 1)
            with act.Fori(0, HEADS // 2) as r:
                for s in range(2):
                    j = 2 * r + s
                    c = lambda n: par[s][:, n:n + 1]
                    act.wait_ge(sem(f"par_here_{s}"), 16 * r + 16)
                    act.wait_ge(pe_sem["f_done"], j + 1)
                    act.activation(sig_f[:, 0:META], B7[:, 0:META], ACT.Sigmoid, bias=c(C_BF))
                    act.activation(sig_f[:, META:TA], BF_[:, 0:T], ACT.Sigmoid, bias=c(C_BF)).then_inc(sem("f_taken"), 1)
                    split_hi(act, j, 4)
                    act.wait_ge(sem("f_ready"), j + 1)
                    act.activation(u[:], f[:], ACT.Ln).then_inc(sem("lf_ready"), 1)
                    act.wait_ge(pe_sem["v_done"], j + 1)
                    act.activation(vTm[:], B7[:, 64:64 + META], ACT.Identity, bias=c(C_BV))
                    act.activation(vT[:], BV_[:, 0:T], ACT.Identity, bias=c(C_BV)).then_inc(sem("v_taken"), 1)
                    split_hi(act, j, 5)
                    act.wait_ge(pe_sem["q_done"], j + 1)
                    act.activation(eq[:], BQ_[:, 0:T], ACT.Sigmoid, bias=c(C_BQ)).then_inc(sem("sigq_ready"), 1)
                    split_hi(act, j, 6)
                    act.wait_ge(pe_sem["vt_done"], j + 1)
                    act.activation(vm[:], B7[0:META, 128:256], ACT.Copy)
                    act.activation(vt[:].rearrange("p t c -> p (t c)"), BV_[:, 0:T], ACT.Copy).then_inc(sem("vt_taken"), 1)
                    act.wait_ge(sem("args_ready"), j + 1)
                    act.activation(eq[:], eq[:], ACT.Exp)
                    act.activation(eb[:], b[:, META:TA], ACT.Exp)
                    for i in range(NSUB):
                        n = SUB * (i + 1)
                        act.activation(k_in[:, i, :, 0:n], k_in[:, i, :, 0:n], ACT.Exp)
                    act.activation(k_st[:], k_st[:], ACT.Exp).then_inc(sem("exps_ready"), 1)
                    act.wait_ge(pe_sem["x_done"], j + 1)
                    act.activation(xr[:, 3:3 + META], B7[:, 16:16 + META], ACT.Identity, bias=c(C_BX))
                    act.activation(xr[:, 3 + META:3 + TA], BX_[:, 0:T], ACT.Identity, bias=c(C_BX)).then_inc(sem("x_taken"), 1)
                    split_hi(act, j, 7)
                    act.wait_ge(pe_sem["o_done"], j + 1)
                    act.activation(sg[0][:], BF_[:, 0:T], ACT.Sigmoid, bias=c(C_BG)).then_inc(sem("sigo_ready"), 1)
                    split_hi(act, j + 1, 0)
                    act.wait_ge(pe_sem["kt_done"], j + 1)
                    act.activation(kTm[:], B7[0:META, 256:384], ACT.Copy)
                    act.activation(kT[:].rearrange("p t c -> p (t c)"), B4[:, 0:T], ACT.Copy).then_inc(sem("kt_taken"), 1)
                    act.wait_ge(pe_sem["l_done"], j + 1)
                    act.activation(gx[:], BQ_[:, 0:T], ACT.Identity, bias=c(C_BL)).then_inc(sem("l_taken"), 1)
                    split_hi(act, j + 1, 1)
                    act.wait_ge(pe_sem["ri_done"], j + 1)
                    act.activation(rr[:, 0:META], B7[:, 32:48], ACT.Sigmoid, bias=c(C_BA))
                    act.activation(rr[:, META:TA], B5[:, 0:T], ACT.Sigmoid, bias=c(C_BA))
                    act.activation(ii[:, 0:META], B7[:, 48:64], ACT.Sigmoid, bias=c(C_BI))
                    act.activation(ii[:, META:TA], B6[:, 0:T], ACT.Sigmoid, bias=c(C_BI)).then_inc(sem("ri_taken"), 1)
                    act.wait_ge(sem("ri_taken"), j + 2)
                    act.wait_ge(sem("gelu_arg"), j + 1)
                    act.activation(gt[:], gt[:], ACT.Sigmoid, scale=GELU_B).then_inc(sem("gelu_sig"), 1)
                    act.activation(la[:], rr[:], ACT.Exp, scale=own[s][:, 2:3])
                    act.activation(pp[:], rr[:], ACT.Tanh, scale=own[s][:, 3:4]).then_inc(sem("a_ready"), 1)
                    act.wait_ge(pe_sem["hg_done"], j + 1)
                    act.activation(sg[1][:], BV_[:, 0:T], ACT.Sigmoid, bias=c(C_BHG)).then_inc(sem("hg_taken"), 1)
                    split_hi(act, j + 1, 2)
                    act.wait_ge(pe_sem["out_done"], j + 1)
                    act.activation(halves(o2)[:, :, 0], of_half(B4), ACT.Square)
                    act.activation(halves(o2)[:, :, 1], of_half(B6), ACT.Square).then_inc(sem("o2_ready"), 1)
                    act.wait_ge(pe_sem["lru_done"], j + 1)
                    act.activation(sg[2][:], BX_[:, 0:T], ACT.Sigmoid, bias=c(C_BLRU)).then_inc(sem("lru_taken"), 1)
                    split_hi(act, j + 1, 3)
                    act.wait_ge(sem("u2_ready"), j + 1)
                    act.activation(pp[:], pp[:], ACT.Sqrt, scale=2.0).then_inc(sem("u_root"), 1)
                    act.wait_ge(pe_sem["rms_done"], j + 1)
                    act.activation(rms[:], B5[:, 0:T], ACT.Sqrt, bias=eps[:], scale=1.0 / P).then_inc(sem("rms_ready"), 1)

        @block.vector
        def _(v):
            N = 42
            st0 = Steps(v, sem("dve2_step"))
            st0.add(v.memset(k_in[:], 0.0))
            st0.add(v.memset(xr[:, 0:3], 0.0))
            v.memset(eps[:], RMS_EPS).then_inc(sem("eps_ready"), 1)
            v.wait_ge(sem("all_cols_here"), 16)
            st0(v.tensor_scalar(lam[:, 5], all_cols[:, 0], -1.0, None, ALU.mult))
            st0.add(v.tensor_scalar(lam[:, 2], lam[:, 5], 0.0, None, ALU.max))
            st0.add(v.tensor_tensor(derived[:, :, 1], all_cols[:, 1], all_cols[:, 2], ALU.subtract))
            st0(v.tensor_tensor(lam[:, 0], lam[:, 5], all_cols[:, 0], ALU.min))
            v.sem_inc(sem("lam_ready"), 1)
            v.wait_ge(sem("elam_ready"), 1)
            e_, t_, s2, ac = lam[:, 1], lam[:, 3], lam[:, 4], lam[:, 5]
            st0.add(v.tensor_scalar(derived[:, :, 1], derived[:, :, 0], -1.0, 1.0, ALU.mult, ALU.add))
            st0(v.tensor_scalar(t_, e_, 2.0, None, ALU.add))
            st0(v.reciprocal(t_, t_))
            st0(v.tensor_tensor(t_, t_, e_, ALU.mult))
            st0(v.tensor_tensor(s2, t_, t_, ALU.mult))
            st0(v.tensor_scalar(ac, s2, 2.0 / 15, 2.0 / 13, ALU.mult, ALU.add))
            for n in (11, 9, 7, 5, 3, 1):
                st0(v.tensor_tensor(ac, ac, s2, ALU.mult))
                st0(v.tensor_scalar(ac, ac, 2.0 / n, None, ALU.add))
            st0(v.tensor_tensor(ac, ac, t_, ALU.mult))
            st0(v.tensor_tensor(ac, ac, lam[:, 2], ALU.add))
            st0.add(v.tensor_scalar(derived[:, :, 2], ac, -8.0, None, ALU.mult))
            st0(v.tensor_scalar(derived[:, :, 3], ac, 8.0, None, ALU.mult))
            v.wait_ge(sem("rows_here"), 32)
            for t in range(TT // 2):
                residual(v, st0, t)
            with v.Fori(0, HEADS // 2) as r:
                for s in range(2):
                    j = 2 * r + s
                    st = Steps(v, sem("dve2_step"), N * j + st0.n)
                    c = lambda n: par[s][:, n:n + 1]
                    v.wait_ge(sem(f"par_here_{s}"), 16 * r + 16)
                    st(v.tensor_copy(own[s][:], derived[:, bass.ds(j, 1)].rearrange("p a n -> p (a n)")))
                    v.wait_ge(sem("f_taken"), j + 1)
                    st(v.tensor_scalar(f[:], sig_f[:], own[s][:, 1:2], own[s][:, 0:1], ALU.mult, ALU.add))
                    v.tensor_scalar(kk[:], f[:], -1.0, 1.0, ALU.mult, ALU.add).then_inc(sem("f_ready"), 1)
                    v.wait_ge(sem("lf_ready"), j + 1)
                    st(v.tensor_tensor_scan(b[:], reset[:], u[:], 0.0, ALU.mult, ALU.add))
                    b4 = b[:, META:TA].rearrange("p (c i s) -> p c i s", c=NCH, i=NSUB)
                    mid = b4[:, :, :, SUB // 2 - 1:SUB // 2]
                    bc = chunked(b[:, META:TA])
                    for i in range(NSUB):
                        n = SUB * (i + 1)
                        st.add(v.tensor_tensor(k_in[:, i, :, 0:n], mid[:, :, i].broadcast_to([P, NCH, n]),
                                               bc[:, :, 0:n], ALU.subtract))
                    st.add(v.tensor_tensor(chunked(k_st[:, META:TA]), bc[:, :, CHUNK - 1:CHUNK].broadcast_to([P, NCH, CHUNK]),
                                           bc, ALU.subtract))
                    st.add(v.tensor_tensor(k_st[:, 0:META], b[:, META - 1:META].broadcast_to([P, META]), b[:, 0:META],
                                           ALU.subtract))
                    v.wait_ge(sem("sigq_ready"), j + 1)
                    v.scalar_tensor_tensor(q[:], BQ_[:, 0:T], c(C_BQ), eq[:], ALU.add, ALU.mult).then_inc(sem("q_taken"), 1)
                    v.wait_ge(sem("q_taken"), j + 1)
                    st.add(v.tensor_tensor(eq[:].rearrange("p (c i s) -> p (c i) s", c=NCH, i=NSUB),
                                           b4.rearrange("p c i s -> p (c i) s"),
                                           mid.rearrange("p c i s -> p (c i) s").broadcast_to([P, NCH * NSUB, SUB]),
                                           ALU.subtract))
                    st.sync()
                    v.sem_inc(sem("args_ready"), 1)
                    v.wait_ge(sem("exps_ready"), j + 1)
                    st.add(v.tensor_tensor(q_in[:], q[:], eq[:], ALU.mult))
                    st.add(v.tensor_tensor(q_st[:], q[:], eb[:], ALU.mult))
                    kc = chunked(kk[:, META:TA])
                    for i in range(NSUB):
                        n = SUB * (i + 1)
                        st.add(v.tensor_tensor(k_in[:, i, :, 0:n], k_in[:, i, :, 0:n], kc[:, :, 0:n], ALU.mult))
                    st(v.tensor_tensor(k_st[:], k_st[:], kk[:], ALU.mult))
                    v.sem_inc(sem("qk_ready"), 1)
                    v.wait_ge(sem("x_taken"), j + 1)
                    st(v.tensor_scalar(xc[:], xr[:, 3:3 + TA], c(C_W3), c(C_CB), ALU.mult, ALU.add))
                    for i in range(3):
                        ins = v.scalar_tensor_tensor(xc[:], xr[:, i:i + TA], c(C_W0 + i), xc[:], ALU.mult, ALU.add)
                        if i < 2:
                            st(ins)
                        else:
                            ins.then_inc(sem("xc_ready"), 1)
                    v.wait_ge(sem("sigo_ready"), j + 1)
                    v.scalar_tensor_tensor(sg[0][:], BF_[:, 0:T], c(C_BG), sg[0][:], ALU.add, ALU.mult).then_inc(sem("o_taken"), 1)
                    v.wait_ge(sem("l_taken"), j + 2)
                    st(v.tensor_tensor(gt[:], gx[:], gx[:], ALU.mult))
                    st(v.tensor_scalar(gt[:], gt[:], GELU_A, 1.0, ALU.mult, ALU.add))
                    v.tensor_tensor(gt[:], gt[:], gx[:], ALU.mult).then_inc(sem("gelu_arg"), 1)
                    v.wait_ge(pe_sem["sc_done"], j + 1)
                    v.tensor_tensor(sc[:], B4[:, 0:TT * CHUNK].rearrange("p (t c) -> p t c", t=TT),
                                    cmask[:].rearrange("p (a c) -> p a c", a=1).broadcast_to([P, TT, CHUNK]),
                                    ALU.mult).then_inc(sem("sc_ready"), 1)
                    v.wait_ge(pe_sem["kv_done"], j + 1)
                    st(v.tensor_copy(S[:, 0], B7[:, 384:512]))
                    for n in range(1, NCH):
                        ins = v.scalar_tensor_tensor(S[:, n], S[:, n - 1], eb[:, n * CHUNK - 1:n * CHUNK],
                                                     (B5, B6)[(n - 1) % 2][:, (n - 1) // 2 * P:((n - 1) // 2 + 1) * P], ALU.mult, ALU.add)
                        if n < NCH - 1:
                            st(ins)
                        else:
                            ins.then_inc(sem("S_ready"), 1)
                    v.wait_ge(sem("ri_taken"), j + 2)
                    v.wait_ge(sem("a_ready"), j + 1)
                    st.add(v.tensor_tensor(ii[:], ii[:], xc[:], ALU.mult))
                    st(v.tensor_scalar(u[:], pp[:], 1.0, None, ALU.add))
                    st(v.reciprocal(u[:], u[:]))
                    v.tensor_tensor(pp[:], pp[:], u[:], ALU.mult).then_inc(sem("u2_ready"), 1)
                    v.wait_ge(sem("gelu_sig"), j + 1)
                    st(v.tensor_tensor(gx[:], gx[:], gt[:], ALU.mult))
                    v.wait_ge(sem("u_root"), j + 1)
                    st(v.tensor_tensor(u[:], pp[:], ii[:], ALU.mult))
                    st(v.tensor_tensor_scan(pp[:], la[:], u[:], 0.0, ALU.mult, ALU.add))
                    st(v.tensor_tensor(gx[:], gx[:], pp[:, META:TA], ALU.mult))
                    v.wait_ge(sem("lru_taken"), j + 2)
                    st(v.tensor_tensor(gx[:], gx[:], sg[2][:], ALU.mult))
                    v.wait_ge(sem("rms_ready"), j + 1)
                    st(v.reciprocal(y[:], rms[:]))
                    for h, bank in enumerate((B4, B6)):
                        st(v.scalar_tensor_tensor(halves(y)[:, :, h], of_half(bank), c(C_NG), halves(y)[:, :, h],
                                                  ALU.mult, ALU.mult))
                    v.wait_ge(sem("o_taken"), j + 2)
                    st(v.tensor_tensor(y[:], y[:], sg[0][:], ALU.mult))
                    v.wait_ge(sem("hg_taken"), j + 2)
                    st(v.tensor_tensor(y[:], y[:], sg[1][:], ALU.mult))
                    v.wait_ge(sem("residual_done"), 1)
                    v.tensor_tensor(merged[:, bass.ds(j, 1), :].rearrange("p a t -> p (a t)"), y[:], gx[:],
                                    ALU.add).then_inc(sem("merged_done"), 1)
                    assert st.n == N, st.n

        @block.gpsimd
        def _(pool):
            gst = Steps(pool, sem("pool_step"))
            pool.wait_ge(sem("rows_here"), 32)
            for t in range(TT // 2, TT):
                residual(pool, gst, t)
            pool.sem_inc(sem("residual_done"), 1)
            with pool.Fori(0, HEADS) as j:
                for n in range(PARTS, GROUPS):
                    split_lo(pool, j, n)
                for n in range(PARTS):
                    split_lo(pool, j + 1, n)
    if stop <= 2:
        dump(nc, sem, dbg, merged[:, :, :])


def load_chunk(sp, a, raw, sem, slot, expert, c):
    src = a["w_gate_up"][expert, :, c] if c < 2 else a["w_down"][expert]
    return sp.dma_start(raw[:, slot], src).then_inc(sem(f"raw_here_{slot}"), 16)


def out_and_route(nc, a, sem, sb, banks, pair, mem, stop, dbg):
    ident, ones, acc, merged, raw = (mem[n] for n in ("ident", "ones", "acc", "merged", "raw"))
    x_hi, x_lo = mem["x_hi"], mem["x_lo"]
    g1 = sb("g1", [P, D])
    b1 = sb("b1", [P, D])
    h1T = sb("h1T", [P, KB, T])
    rw = sb("rw", [P, KB, E])
    rbias = sb("rbias", [P, E])
    ws_gu = sb("ws_gu", [P, KB, 2 * F])
    ws_dn = sb("ws_dn", [P, 2, D])
    aT = sb("aT", [P, 2, T])
    stats = sb("stats1", [P, TT, 2, 6])
    mv = sb("mv1", [P, TT, 2])
    rs = sb("rs1", [P, TT, 2])
    before = sb("before", [P, P])
    before2 = sb("before2", [P, P])
    onehot = sb("onehot", [P, ITEMS])
    steps64 = sb("steps64", [P, 12])
    steps4 = sb("steps4", [P, 12])
    e_col = sb("e_col", [P, 1])
    iota = mem["iota"]

    with nc.Block() as block:
        @block.sync
        def _(sp):
            sp.dma_start(g1[:], a["norm_rows"][2:3].broadcast_to([P, D])).then_inc(sem("ln1_here"), 16)
            sp.dma_start(b1[:], a["norm_rows"][3:4].broadcast_to([P, D])).then_inc(sem("ln1_here"), 16)
            for t, n in ((rw, "router_w"), (rbias, "router_bias"), (before, "before"), (before2, "before2"),
                         (steps64, "steps64"), (steps4, "steps4"), (e_col, "e_col"), (iota, "iota"),
                         (onehot, "onehot")):
                src = a[n].broadcast_to([P, E]) if n == "router_bias" else a[n]
                sp.dma_start(t[:], src).then_inc(sem("route_here"), 16)
            sp.dma_start(ws_gu[:], a["ws_gate_up"]).then_inc(sem("shared_here"), 16)
            sp.dma_start(ws_dn[:], a["ws_down"]).then_inc(sem("shared_here"), 16)
            for n in range(RAW - 2):
                load_chunk(sp, a, raw, sem, n, n // CHUNKS, n % CHUNKS)

        @block.tensor
        def _(pe):
            for t in range(EARLY, TT):
                pe.wait_ge(sem("mix_taken"), t - 1)
                for n in range(2):
                    for j in range(HEADS):
                        last = project_out(pe, mem, banks, t, n, j)
                last.then_inc(sem("mix_done"), 1)
            for t in range(TT):
                pe.wait_ge(sem("h1_ready"), t + 1)
                if t >= 2:
                    pe.wait_ge(sem("h1T_taken"), t - 1)
                for k in range(KB):
                    last = pe.transpose(pair[2 + t % 2][:, k * P:(k + 1) * P], acc[:, t, k::KB], ident[:])
                last.then_inc(sem("h1T_done"), 1)

        @block.vector
        def _(v):
            st = Steps(v, sem("ln1_step"))

            def normed(t):
                v.wait_ge(sem("std1_ready"), t + 1)
                st(v.reciprocal(rs[:, t, 0:1], rs[:, t, 1:2]))
                st(v.tensor_scalar(acc[:, t], acc[:, t], mv[:, t, 0:1], rs[:, t, 0:1], ALU.subtract, ALU.mult))
                st(v.tensor_tensor(acc[:, t], acc[:, t], g1[:], ALU.mult))
                v.tensor_tensor(acc[:, t], acc[:, t], b1[:], ALU.add).then_inc(sem("h1_ready"), 1)

            def mixed(t):
                v.wait_ge(sem("mix_done"), t + 1)
                v.scalar_tensor_tensor(acc[:, t], acc[:, t], ALPHA, pair[t % 2][:, :], ALU.mult, ALU.add)\
                 .then_inc(sem("mix_taken"), 1)
                v.wait_ge(sem("mix_taken"), t + 1)
                st.add(v.bn_stats(stats[:, t, 0], acc[:, t, 0:512]))
                st(v.bn_stats(stats[:, t, 1], acc[:, t, 512:1024]))
                st(v.bn_aggr(mv[:, t], stats[:, t]))
                v.tensor_scalar(rs[:, t, 0:1], mv[:, t, 1:2], LN_EPS, None, ALU.add).then_inc(sem("var1_ready"), 1)

            for t in range(EARLY):
                mixed(t)
            v.wait_ge(sem("ln1_here"), 32)
            for t in range(TT):
                normed(t)
                if t + EARLY < TT:
                    mixed(t + EARLY)

        @block.gpsimd
        def _(pool):
            for t in range(TT):
                pool.wait_ge(sem("x_hi_ready"), t + 1)
                pool.tensor_tensor(x_lo[:, t], acc[:, t].rearrange("p (q k) -> p k q", k=KB), x_hi[:, t].bitcast(F32),
                                   ALU.subtract)

        @block.scalar
        def _(act):
            def root(t):
                act.wait_ge(sem("var1_ready"), t + 1)
                act.activation(rs[:, t, 1:2], rs[:, t, 0:1], ACT.Sqrt).then_inc(sem("std1_ready"), 1)

            for t in range(EARLY):
                root(t)
            for t in range(TT):
                act.wait_ge(sem("h1_ready"), t + 1)
                act.activation(x_hi[:, t], acc[:, t].rearrange("p (q k) -> p k q", k=KB), ACT.Copy)\
                   .then_inc(sem("x_hi_ready"), 1)
                if t + EARLY < TT:
                    root(t + EARLY)
                act.wait_ge(sem("h1T_done"), t + 1)
                act.activation(h1T[:, :, t * P:(t + 1) * P], pair[2 + t % 2][:, :].rearrange("p (k c) -> p k c", k=KB),
                               ACT.Copy).then_inc(sem("h1T_taken"), 1)

    sc = sb("scores", [P, TT, E])
    bs = sb("biased", [P, TT, E])
    top8 = sb("top8", [P, TT, 8])
    above = sb("above", [P, TT, E])
    tie = sb("tie", [P, TT, E])
    ties = sb("ties", [P, TT, E])
    room = sb("room", [P, TT])
    chosen = sb("chosen", [P, TT, 2, E])
    norm = sb("norm", [P, TT, 2])
    pw = sb("pw", [P, TT, 2 * E])
    pwT = sb("pwT", [P, TT, P])
    cnt = sb("cnt", [P, 4])
    tmp = sb("tmp", [P, 12])
    d1 = sb("d1", [P, EXTRA])
    d2 = sb("d2", [P, EXTRA])
    base = sb("base", [P, ITEMS])
    left1 = sb("left1", [P, TT, ITEMS])
    left2 = sb("left2", [P, TT, ITEMS])
    q2 = sb("q2", [1, 16])
    with nc.Block() as block:
        R, PO, W_, SM = banks[0], banks[1], banks[6], banks[7]

        @block.sync
        def _(sp):
            for n in range(RAW - 2, RAW):
                load_chunk(sp, a, raw, sem, n, n // CHUNKS, n % CHUNKS)

        @block.tensor
        def _(pe):
            pe.wait_ge(sem("route_here"), 16 * 9)
            for t in range(TT):
                for k in range(KB):
                    last = pe.matmul(R[:, t * E:(t + 1) * E], h1T[:, k, t * P:(t + 1) * P], rw[:, k],
                                     start=(k == 0), stop=(k == KB - 1))
            last.then_inc(sem("logits_done"), 1)
            pe.wait_ge(sem("shared_here"), 32)
            for m in range(4):
                for k in range(KB):
                    last = pe.matmul(banks[2 + m][:, :], ws_gu[:, k, m * P:(m + 1) * P], h1T[:, k],
                                     start=(k == 0), stop=(k == KB - 1))
                last.then_inc(sem("shared_up_done"), 1)
            pe.wait_ge(sem("chosen_ready"), 1)
            for t in range(TT):
                for u in range(t):
                    pe.matmul(PO[:, t * E:(t + 1) * E], ones[:], chosen[:, u, 0], start=(u == 0), stop=False)
                last = pe.matmul(PO[:, t * E:(t + 1) * E], before[:], chosen[:, t, 0], start=(t == 0), stop=True)
            last.then_inc(sem("place_done"), 1)
            for t in range(TT):
                last = pe.matmul(SM[:, 0:1], chosen[:, t].rearrange("p a e -> p (a e)"), ones[:, 0:1],
                                 start=(t == 0), stop=(t == TT - 1))
            last.then_inc(sem("count_done"), 1)
            pe.wait_ge(sem("a_shared_ready"), 2)
            for t in range(TT):
                if t == 1:
                    pe.wait_ge(sem("further_ready"), 1)
                    pe.matmul(SM[:, 1:2], before2[:], cnt[:, 1:2], start=True, stop=True).then_inc(sem("start_done"), 1)
                if t == 2:
                    pe.wait_ge(sem("pw_ready"), 1)
                    for u in range(TT):
                        last = pe.transpose(PO[:, u * P:(u + 1) * P], pw[:, u], ident[:])
                    last.then_inc(sem("pwT_done"), 1)
                if t >= 2:
                    pe.wait_ge(sem("shared_taken"), t - 1)
                for n in range(2):
                    for j in range(2):
                        last = pe.matmul(banks[2 + 2 * (t % 2) + n][:, :], aT[:, j, t * P:(t + 1) * P],
                                         ws_dn[:, j, n * 512:(n + 1) * 512], start=(j == 0), stop=(j == 1))
                last.then_inc(sem("shared_done"), 1)
            pe.wait_ge(sem("items_ready"), 1)
            pe.wait_ge(sem("pwT_ready"), 1)
            for t in range(TT):
                o = R[:, t * ITEMS:(t + 1) * ITEMS]
                pe.matmul(o, pwT[0:E, t], onehot[0:E], start=True, stop=False)
                pe.matmul(o, ones[0:E], base[0:E], start=False, stop=True)
            for t in range(TT):
                pe.matmul(W_[:, t * ITEMS:(t + 1) * ITEMS], pwT[E:P, t], onehot[E:P], start=True, stop=True)
            pe.matmul(SM[0:1, 0:ITEMS], e_col[0:E], onehot[0:E], start=True, stop=True)
            pe.matmul(SM[0:1, ITEMS:ITEMS + 1], ones[0:E, 0:1], cnt[0:E, 1:2], start=True, stop=True)\
              .then_inc(sem("tables_done"), 1)

        @block.scalar
        def _(act):
            act.wait_ge(sem("logits_done"), 1)
            act.activation(sc[:].rearrange("p t e -> p (t e)"), R[:, 0:TT * E], ACT.Sigmoid).then_inc(sem("scores_ready"), 1)
            for j in range(2):
                act.wait_ge(sem("shared_up_done"), j + 1)
                act.activation(aT[:, j], banks[2 + j][:, :], ACT.Silu).then_inc(sem("silu_ready"), 1)
            act.wait_ge(sem("pwT_done"), 1)
            act.activation(pwT[:].rearrange("p t c -> p (t c)"), PO[:, :], ACT.Copy).then_inc(sem("pwT_ready"), 1)

        @block.vector
        def _(v):
            st = Steps(v, sem("route_step"))
            each = lambda x, n=E: x.broadcast_to([P, TT, n])
            v.wait_ge(sem("route_here"), 16 * 9)
            v.wait_ge(sem("scores_ready"), 1)
            st(v.tensor_tensor(bs[:], sc[:], each(rbias[:].rearrange("p (a e) -> p a e", a=1)), ALU.add))
            for t in range(TT):
                st.add(v.max(top8[:, t], bs[:, t]))
            st.sync()
            sixth = top8[:, :, TOP_K - 1:TOP_K]
            st(v.tensor_tensor(above[:], bs[:], each(sixth), ALU.is_gt))
            st(v.tensor_tensor(tie[:], bs[:], each(sixth), ALU.is_equal))
            st(v.tensor_reduce(room[:], above[:], AX, ALU.add))
            st(v.tensor_scalar(room[:], room[:], -1.0, float(TOP_K), ALU.mult, ALU.add))
            for t in range(TT):
                st.add(v.tensor_tensor_scan(ties[:, t], ones[:, 0:E], tie[:, t], 0.0, ALU.mult, ALU.add))
            st.sync()
            st(v.tensor_tensor(ties[:], ties[:], each(room[:].rearrange("p (t a) -> p t a", a=1)), ALU.is_le))
            st(v.tensor_tensor(ties[:], ties[:], tie[:], ALU.mult))
            st(v.tensor_tensor(chosen[:, :, 0], ties[:], above[:], ALU.add))
            v.tensor_copy(chosen[:, :, 1], chosen[:, :, 0]).then_inc(sem("chosen_ready"), 1)
            st(v.tensor_tensor(sc[:], sc[:], chosen[:, :, 0], ALU.mult))
            st(v.tensor_reduce(norm[:, :, 0], sc[:], AX, ALU.add))
            st(v.reciprocal(norm[:, :, 1], norm[:, :, 0]))
            st(v.tensor_scalar(norm[:, :, 1], norm[:, :, 1], ROUTED_SCALE, None, ALU.mult))
            st(v.tensor_tensor(pw[:, :, E:2 * E], sc[:], each(norm[:, :, 1:2]), ALU.mult))
            v.wait_ge(sem("place_done"), 1)
            v.scalar_tensor_tensor(pw[:, :, 0:E], PO[:, 0:TT * E].rearrange("p (t e) -> p t e", t=TT), FAR,
                                   chosen[:, :, 0], ALU.add, ALU.mult).then_inc(sem("pw_ready"), 1)
            v.wait_ge(sem("count_done"), 1)
            st(v.tensor_copy(cnt[:, 0:1], SM[:, 0:1]))
            st(v.tensor_scalar(tmp[:], steps64[:], cnt[:, 0:1], None, ALU.is_lt))
            v.tensor_reduce(cnt[:, 1:2], tmp[:], AX, ALU.add).then_inc(sem("further_ready"), 1)
            for j in range(2):
                v.wait_ge(sem("silu_ready"), j + 1)
                v.wait_ge(sem("shared_up_done"), j + 3)
                v.tensor_tensor(aT[:, j], aT[:, j], banks[4 + j][:, :], ALU.mult).then_inc(sem("a_shared_ready"), 1)
            v.wait_ge(sem("start_done"), 1)
            st(v.tensor_copy(cnt[:, 2:3], SM[:, 1:2]))
            st(v.tensor_scalar(d1[:], iota[:, 0:EXTRA], cnt[:, 2:3], None, ALU.subtract))
            st.add(v.memset(base[:], 0.0))
            st(v.tensor_scalar(d2[:], d1[:], cnt[:, 1:2], None, ALU.is_lt))
            st(v.scalar_tensor_tensor(onehot[:, E:ITEMS], d1[:], 0.0, d2[:], ALU.is_ge, ALU.mult))
            st(v.tensor_scalar(d1[:], d1[:], -float(SLOTS), -float(SLOTS), ALU.mult, ALU.add))
            v.tensor_tensor(base[:, E:ITEMS], d1[:], onehot[:, E:ITEMS], ALU.mult).then_inc(sem("items_ready"), 1)
            for t in range(TT):
                v.wait_ge(sem("shared_done"), t + 1)
                v.scalar_tensor_tensor(acc[:, t], acc[:, t], ALPHA, pair[1 + t % 2][:, :], ALU.mult, ALU.add)\
                 .then_inc(sem("shared_taken"), 1)
            st.add(v.memset(mem["slot_of"][:, ITEMS:], -FAR))
            v.wait_ge(sem("tables_done"), 1)
            st.add(v.tensor_scalar(mem["slot_of"][:, 0:ITEMS].rearrange("p i t -> p t i"),
                                   R[:, 0:TT * ITEMS].rearrange("p (t i) -> p t i", t=TT), FAR, None, ALU.subtract))
            w3 = mem["weight_of"][:].rearrange("p i t n -> p t i n")
            left = [W_[:, 0:TT * ITEMS].rearrange("p (t i) -> p t i", t=TT), left1[:], left2[:]]
            for n in range(3):
                st(v.tensor_copy(w3[:, :, :, n], left[n]))
                if n < 2:
                    st(v.tensor_tensor(left[n + 1], left[n], w3[:, :, :, n], ALU.subtract))
            st.add(v.tensor_copy(mem["expert_of"][:], SM[0:1, 0:ITEMS]))
            st(v.tensor_copy(q2[:, 12:13], SM[0:1, ITEMS:ITEMS + 1]))
            st(v.tensor_scalar(q2[:, 0:12], steps4[0:1], q2[:, 12:13], None, ALU.is_lt))
            st(v.tensor_reduce(q2[:, 13:14], q2[:, 0:12], AX, ALU.add))
            st(v.tensor_scalar(q2[:, 14:15], q2[:, 13:14], float(E // QUAD), None, ALU.add))
            st(v.tensor_copy(mem["quads"][:], q2[:, 14:15]))

    if stop <= 3:
        dump(nc, sem, dbg, acc[:, :, :])


def experts(nc, a, sem, sb, banks, pair, mem, stop, dbg):
    ident, acc, raw, iota = (mem[n] for n in ("ident", "acc", "raw", "iota"))
    x_parts, slot_of, weight_of = (mem["x_hi"], mem["x_lo"]), mem["slot_of"], mem["weight_of"]
    split = [sb(f"split{n}", [P, 2, CHUNK_W], F32R) for n in range(CHUNKS)]
    xg = sb("xg", [P, QUAD, KB, 2, SLOTS], F32R)
    gu = sb("gu", [P, 2 * F])
    act_s = sb("act_s", [P, 2, SLOTS])
    act_a = sb("act_a", [P, 2, SLOTS])
    a_in = sb("a_in", [P, 2, 2, SLOTS], F32R)
    y_rest = sb("y_rest", [P, D])
    Sr = sb("Sr", [P, TT, QUAD, SLOTS], F32R)
    Sb = sb("Sb", [P, TT, QUAD, 2, SLOTS], BF16)
    ST = [sb(f"ST{n}", [P, TT, P], F32R) for n in range(QUAD)]
    wcol = sb("wcol", [P, QUAD])
    y = [sb(f"y{n}", [P, D], F32R) for n in range(QUAD)]
    two = sb("two", [P, SLOTS])
    ident_b = sb("ident_b", [P, P], BF16)
    GU, TR, WC, Y = banks[0], banks[1], banks[6], (pair[2], pair[3])
    TURN = banks[2:4]
    SUM = banks[4:8]
    XG = (banks[6], banks[7], banks[2], banks[3])
    LD = 1216
    flat = lambda x: x.rearrange("p a s -> p (a s)")

    def quads(eng):
        return eng.value_load(mem["quads"][0:1, 0:1], min_val=E // QUAD, max_val=QUADS_MAX)

    with nc.Block() as block:
        @block.sync
        def _(sp):
            sp.dma_start(two[:], a["two"]).then_inc(sem("two_here"), 16)

            def load(i, u, expert):
                for c in range(CHUNKS):
                    sp.wait_ge(sem(f"hi{c}_ready"), i - 1)
                    sp.wait_ge(sem(f"lo{c}_dve"), i - 1)
                    sp.wait_ge(sem(f"lo{c}_pool"), i - 1)
                    sp.wait_ge(sem("two_here"), 16)
                    load_chunk(sp, a, raw, sem, (CHUNKS * u + c) % RAW, expert, c)

            for i in range(2, QUAD):
                load(i, i, i)
            n_quads = quads(sp)
            with sp.Fori(1, n_quads) as q:
                for u in range(QUAD):
                    e = sp.value_load(mem["expert_of"][0:1, bass.ds(QUAD * q + u, 1)], min_val=0, max_val=E - 1)
                    load(QUAD * q + u, u, e)
            for c in range(2):
                sp.wait_ge(sem(f"raw_here_{c}"), 32 * n_quads)
                sp.sem_inc(sem(f"raw_here_{c}"), 16)

        @block.tensor
        def _(pe):
            def split_here(i, c):
                for name in (f"hi{c}_ready", f"lo{c}_dve", f"lo{c}_pool"):
                    pe.wait_ge(sem(name), i + 1)

            def gather(r):
                pe.wait_ge(sem("S_half"), r + 1)
                for k in range(KB):
                    if k >= 4:
                        pe.wait_ge(sem("xg_act" if k % 2 == 0 else "xg_dve"), 4 * r + k // 2 - 1)
                    for part in range(2):
                        for t in range(TT):
                            last = pe.matmul(XG[k % 4][:, part * 256:(part + 1) * 256], x_parts[part][:, t, k],
                                             Sr[:, t].rearrange("p u s -> p (u s)"), start=(t == 0), stop=(t == TT - 1))
                    last.then_inc(sem("x_done"), 1)

            def gate_up(i, u):
                for c in range(2):
                    split_here(i, c)
                    for k in range(KB // 2):
                        for part in range(2):
                            last = pe.matmul(GU[:, :], flat(xg[:, u, (KB // 2) * c + k]),
                                             split[c][:, part, k * 2 * F:(k + 1) * 2 * F],
                                             start=(c == 0 and k == 0 and part == 0),
                                             stop=(c == 1 and k == KB // 2 - 1 and part == 1))
                    last.then_inc(sem("gate_up_half"), 1)

            def turn(i):
                pe.wait_ge(sem("gu_ready"), i + 1)
                for m in range(4):
                    last = pe.matmul(TR[:, m * SLOTS:(m + 1) * SLOTS], gu[:, m * P:(m + 1) * P], two[:],
                                     start=True, stop=True)
                last.then_inc(sem("tr_done"), 1)

            def down(i, u):
                pe.wait_ge(sem("a_in_ready"), i + 1)
                split_here(i, 2)
                if u >= 2:
                    pe.wait_ge(sem("y_ready"), i)
                for n in range(2):
                    for j in range(2):
                        for part in range(2):
                            last = pe.matmul(Y[u % 2][:, n * 512:(n + 1) * 512], flat(a_in[:, j]),
                                             split[2][:, part, j * D + n * 512:j * D + (n + 1) * 512],
                                             start=(j == 0 and part == 0), stop=(j == 1 and part == 1))
                last.then_inc(sem("y_done"), 1)

            def scatter(q, g0, g1):
                for g in range(g0, g1):
                    t, n = g // 2, g % 2
                    pe.wait_ge(sem("sum_free"), 2 * TT * q + g + 1)
                    for u in range(QUAD):
                        last = pe.matmul(SUM[g % 4][:, :], ST[u][:, t], y[u][:, n * 512:(n + 1) * 512],
                                         start=(u == 0), stop=(u == QUAD - 1))
                    last.then_inc(sem("sum_done"), 1)

            def slots_turned(q):
                pe.wait_ge(sem("S_built"), q + 1)
                pe.wait_ge(sem("sum_free"), 2 * TT * q + 2 * TT + 4)
                for u in range(QUAD):
                    for t in range(TT):
                        at = (u % 2) * 512 + t * P
                        pe.transpose(TURN[u // 2].bitcast(BF16)[:, at:at + P], flat(Sb[:, t, u]), ident_b[:])
                        last = pe.matmul(WC[:, (u * TT + t) * 3:(u * TT + t) * 3 + 3], flat(Sb[:, t, u]),
                                         weight_of[:, bass.ds(QUAD * q + u, 1), t], start=True, stop=True)
                last.then_inc(sem("st_done"), 1)

            pe.wait_ge(sem("two_here"), 16)
            for name in ("y_done", "ST_act", "ST_dve"):
                pe.sem_inc(sem(name), 1)
            gather(0)
            n_quads = quads(pe)
            with pe.Fori(0, n_quads) as q:
                i = QUAD * q
                pe.wait_ge(sem("xg_act"), 4 * q + 4)
                pe.wait_ge(sem("xg_dve"), 4 * q + 4)
                gate_up(i, 0)
                pe.wait_ge(sem("y_ready"), QUAD * q + 1)
                pe.wait_ge(sem("ST_act"), q + 1)
                pe.wait_ge(sem("ST_dve"), q + 1)
                scatter(q, 0, 4)
                turn(i)
                scatter(q, 4, 8)
                gate_up(i + 1, 1)
                slots_turned(q)
                down(i, 0)
                turn(i + 1)
                gate_up(i + 2, 2)
                pe.wait_ge(sem("ST_dve"), q + 2)
                down(i + 1, 1)
                turn(i + 2)
                gate_up(i + 3, 3)
                down(i + 2, 2)
                turn(i + 3)
                pe.wait_ge(sem("ST_act"), q + 2)
                pe.wait_ge(sem("y_ready"), i + 3)
                gather(q + 1)
                pe.wait_ge(sem("xg_act"), 4 * q + 7)
                pe.wait_ge(sem("xg_dve"), 4 * q + 7)
                down(i + 3, 3)
            pe.wait_ge(sem("y_ready"), QUAD * n_quads + 1)
            scatter(n_quads, 0, 8)

        def here(eng, q, u, c):
            n = CHUNKS * u + c
            eng.wait_ge(sem(f"raw_here_{n % RAW}"), 16 * (2 * q + n // RAW) + 16)
            return raw[:, n % RAW]

        def xg_out(k):
            return xg[:, :, k].rearrange("p u a s -> p a u s")

        def xg_in(k):
            return XG[k % 4].rearrange("p (a u s) -> p a u s", a=2, u=QUAD)

        @block.scalar
        def _(act):
            def split_hi(q, u, c):
                act.activation(split[c][:, 0], here(act, q, u, c), ACT.Copy).then_inc(sem(f"hi{c}_ready"), 1)

            def y_first(q, i, u):
                act.wait_ge(sem("wcol_ready"), q + 1)
                act.wait_ge(sem("y_done"), i + 2)
                act.activation(y[u][0:SLOTS], Y[u % 2][0:SLOTS, :], ACT.Copy, scale=wcol[0:SLOTS, u:u + 1])\
                   .then_inc(sem("y_hi_ready"), 1)

            def take_x(r, k0, k1):
                for k in range(k0, k1, 2):
                    act.wait_ge(sem("x_done"), KB * r + k + 1)
                    act.activation(xg_out(k), xg_in(k), ACT.Copy).then_inc(sem("xg_act"), 1)

            for c in range(2):
                split_hi(0, 0, c)
            take_x(0, 0, KB)
            with act.Fori(0, quads(act)) as q:
                for u in range(QUAD):
                    i = QUAD * q + u
                    act.wait_ge(sem("gate_up_half"), 2 * i + 1)
                    split_hi(q, u + 1, 0)
                    act.wait_ge(sem("gate_up_half"), 2 * i + 2)
                    act.activation(gu[:], GU[:, :], ACT.Copy).then_inc(sem("gu_ready"), 1)
                    split_hi(q, u + 1, 1)
                    if u == 1:
                        act.wait_ge(sem("st_done"), q + 1)
                        for m in range(2):
                            ins = act.activation(ST[m][:].rearrange("p t c -> p (t c)"),
                                                 TURN[0].bitcast(BF16)[:, m * 512:(m + 1) * 512], ACT.Copy)
                        ins.then_inc(sem("ST_act"), 1)
                    act.wait_ge(sem("y_done"), i + 1)
                    split_hi(q, u, 2)
                    if 0 < u < QUAD - 1:
                        y_first(q, i - 1, u - 1)
                    act.wait_ge(sem("tr_done"), i + 1)
                    act.activation(flat(act_s[:]), TR[:, 0:2 * SLOTS], ACT.Silu).then_inc(sem("silu2_ready"), 1)
                take_x(q + 1, 0, 4)
                y_first(q, QUAD * q + QUAD - 2, QUAD - 2)
                take_x(q + 1, 4, KB)
                y_first(q, QUAD * q + QUAD - 1, QUAD - 1)

        def split_lo(eng, q, u, c, cols, name):
            eng.wait_ge(sem(f"hi{c}_ready"), QUAD * q + u + 1)
            n = CHUNKS * u + c
            eng.tensor_tensor(split[c][:, 1, cols], raw[:, n % RAW, cols], split[c][:, 0, cols].bitcast(F32),
                              ALU.subtract).then_inc(sem(name), 1)

        @block.vector
        def _(v):
            def build(r):
                at = slot_of[:, bass.ds(QUAD * r, QUAD)].rearrange("p u t -> p t u")\
                    .rearrange("p t (u s) -> p t u s", s=1)
                row = iota[:].rearrange("p (t u s) -> p t u s", t=1, u=1)
                v.tensor_tensor(Sr[:], row.broadcast_to([P, TT, QUAD, SLOTS]), at.broadcast_to([P, TT, QUAD, SLOTS]),
                                ALU.is_equal).then_inc(sem("S_half"), 1)

            def lo(q, u, c):
                split_lo(v, q, u, c, slice(0, LD), f"lo{c}_dve")

            def take_x(r, k0, k1):
                for k in range(k0, k1, 2):
                    v.wait_ge(sem("x_done"), KB * r + k + 1)
                    v.tensor_copy(xg_out(k), xg_in(k)).then_inc(sem("xg_dve"), 1)

            def y_second(i, u):
                v.wait_ge(sem("y_hi_ready"), i + 1)
                v.scalar_tensor_tensor(y_rest[SLOTS:P], Y[u % 2][0:SLOTS, :], wcol[0:SLOTS, u:u + 1],
                                       y[u][0:SLOTS].bitcast(F32), ALU.mult, ALU.subtract).then_inc(sem("y_rest"), 1)
                v.wait_ge(sem("y_rest"), i + 1)
                v.scalar_tensor_tensor(y[u][SLOTS:P], Y[u % 2][SLOTS:P, :], wcol[SLOTS:P, u:u + 1],
                                       y_rest[SLOTS:P], ALU.mult, ALU.add).then_inc(sem("y_ready"), 1)

            def add_up(q, g0, g1):
                for g in range(g0, g1):
                    v.wait_ge(sem("sum_done"), 2 * TT * q + g + 1)
                    part = acc[:, g // 2, (g % 2) * 512:(g % 2 + 1) * 512]
                    v.tensor_tensor(part, part, SUM[g % 4][:, :], ALU.add).then_inc(sem("sum_free"), 1)

            build(0)
            v.tensor_copy(ident_b[:], ident[:])
            v.sem_inc(sem("sum_free"), 4)
            for c in range(2):
                lo(0, 0, c)
            take_x(0, 1, KB)
            n_quads = quads(v)
            with v.Fori(0, n_quads) as q:
                for u in range(QUAD):
                    i = QUAD * q + u
                    lo(q, u + 1, 0)
                    if u == 0:
                        add_up(q, 0, 4)
                    lo(q, u + 1, 1)
                    if u == 0:
                        add_up(q, 4, 8)
                    if u == 1:
                        v.wait_ge(sem("st_done"), q + 1)
                        v.tensor_reduce(wcol[:], WC[:, 0:QUAD * TT * 3].rearrange("p (u n) -> p u n", u=QUAD), AX,
                                        ALU.add).then_inc(sem("wcol_ready"), 1)
                        for m in range(2):
                            ins = v.tensor_copy(ST[2 + m][:].rearrange("p t c -> p (t c)"),
                                                TURN[1].bitcast(BF16)[:, m * 512:(m + 1) * 512])
                        ins.then_inc(sem("ST_dve"), 1)
                        build(q + 1)
                    lo(q, u, 2)
                    v.wait_ge(sem("silu2_ready"), i + 1)
                    v.tensor_tensor(flat(act_a[:]), flat(act_s[:]), TR[:, 2 * SLOTS:4 * SLOTS], ALU.mult)\
                     .then_inc(sem("aa_ready"), 1)
                    v.wait_ge(sem("aa_ready"), i + 1)
                    v.tensor_copy(a_in[:, :, 0], act_a[:]).then_inc(sem("a_hi_ready"), 1)
                    v.wait_ge(sem("a_hi_ready"), i + 1)
                    v.tensor_tensor(a_in[:, :, 1], act_a[:], a_in[:, :, 0].bitcast(F32), ALU.subtract)\
                     .then_inc(sem("a_in_ready"), 1)
                    if 0 < u < QUAD - 1:
                        y_second(i - 1, u - 1)
                take_x(q + 1, 1, 4)
                y_second(QUAD * q + QUAD - 2, QUAD - 2)
                take_x(q + 1, 5, KB)
                y_second(QUAD * q + QUAD - 1, QUAD - 1)
            add_up(n_quads, 0, 8)

        @block.gpsimd
        def _(pool):
            def lo(q, u, c):
                split_lo(pool, q, u, c, slice(LD, CHUNK_W), f"lo{c}_pool")

            def copies(r):
                for m in range(2):
                    ins = pool.tensor_copy(Sb[:, :, :, m], Sr[:].bitcast(F32))
                ins.then_inc(sem("S_built"), 1)

            pool.wait_ge(sem("S_half"), 1)
            copies(0)
            for c in range(2):
                lo(0, 0, c)
            for n in range(QUAD):
                pool.memset(y[n][:].bitcast(F32), 0.0)
                ins = pool.memset(ST[n][:].bitcast(F32), 0.0)
            ins.then_inc(sem("y_ready"), 1)
            with pool.Fori(0, quads(pool)) as q:
                for u in range(QUAD):
                    lo(q, u + 1, 0)
                    lo(q, u + 1, 1)
                    if u == 2:
                        pool.wait_ge(sem("S_half"), q + 2)
                        pool.wait_ge(sem("st_done"), q + 1)
                    lo(q, u, 2)
                    if u == 2:
                        copies(q + 1)


def output_norm(nc, a, sem, sb, mem, out):
    acc = mem["acc"]
    g2 = sb("g2", [P, D])
    b2 = sb("b2", [P, D])
    stats = sb("stats2", [P, TT, 2, 6])
    mv = sb("mv2", [P, TT, 2])
    rs = sb("rs2", [P, TT, 2])
    with nc.Block() as block:
        @block.sync
        def _(sp):
            sp.dma_start(g2[:], a["norm_rows"][4:5].broadcast_to([P, D])).then_inc(sem("ln2_here"), 16)
            sp.dma_start(b2[:], a["norm_rows"][5:6].broadcast_to([P, D])).then_inc(sem("ln2_here"), 16)
            for t in range(TT):
                sp.wait_ge(sem("out_ready"), t + 1)
                sp.dma_start(out[t * P:(t + 1) * P], acc[:, t]).then_inc(sem("stored"), 16)
            sp.wait_ge(sem("stored"), 16 * TT)

        @block.scalar
        def _(act):
            for t in range(TT):
                act.wait_ge(sem("var2_ready"), t + 1)
                act.activation(rs[:, t, 1:2], rs[:, t, 0:1], ACT.Sqrt).then_inc(sem("std2_ready"), 1)

        @block.vector
        def _(v):
            st = Steps(v, sem("ln2_step"))

            def stats_of(t):
                st(v.bn_stats(stats[:, t, 0], acc[:, t, 0:512]))
                st(v.bn_stats(stats[:, t, 1], acc[:, t, 512:1024]))
                st(v.bn_aggr(mv[:, t], stats[:, t]))
                v.tensor_scalar(rs[:, t, 0:1], mv[:, t, 1:2], LN_EPS, None, ALU.add).then_inc(sem("var2_ready"), 1)

            stats_of(0)
            for t in range(TT):
                if t + 1 < TT:
                    stats_of(t + 1)
                v.wait_ge(sem("std2_ready"), t + 1)
                st(v.reciprocal(rs[:, t, 0:1], rs[:, t, 1:2]))
                st(v.tensor_scalar(acc[:, t], acc[:, t], mv[:, t, 0:1], rs[:, t, 0:1], ALU.subtract, ALU.mult))
                v.wait_ge(sem("ln2_here"), 32)
                st(v.tensor_tensor(acc[:, t], acc[:, t], g2[:], ALU.mult))
                v.tensor_tensor(acc[:, t], acc[:, t], b2[:], ALU.add).then_inc(sem("out_ready"), 1)


def dump(nc, sem, dbg, ap):
    with nc.Block() as block:
        @block.sync
        def _(sp):
            sp.dma_start(dbg, ap).then_inc(sem("dumped"), 16)
            sp.wait_ge(sem("dumped"), 16)


def layout(i):
    w = {}
    w["x"] = i["x"][0]
    w["meta"] = i["meta_tokens"]
    w["w_in"] = i["w_in"][0].reshape(P, KB, GROUPS, HEADS, P).transpose(3, 0, 2, 1, 4)[:, :, list(W_ORDER)]
    w["w_in"] = np.concatenate([w["w_in"].reshape(HEADS, P, GROUPS * D),
                                i["w_out"][0].reshape(1, HEADS, P, D).transpose(0, 2, 1, 3).reshape(1, P, HEADS * D)])
    w["w_in"] = w["w_in"].reshape(HEADS + 1, P, PAIRS, 2, D)
    b = i["b_in"][0].reshape(GROUPS, HEADS, P)
    lb = i["hg_lb_logits"].reshape(2, HEADS, P)
    ng = np.broadcast_to(i["hg_norm_g"].reshape(1, P), (HEADS, P))
    cw = i["conv_w"][0].reshape(CONV_W, HEADS, P)
    h = lambda n: i[n][0].reshape(HEADS, P)
    w["head_cols"] = np.stack([b[GQ], b[GF], b[GV], b[GO], b[GX], b[GL], b[GHG], b[GLRU], ng, cw[0], cw[1],
                               cw[2], cw[3], h("conv_b"), h("lru_ba"), h("lru_bx")], axis=2)
    w["all_cols"] = np.stack([h("lru_lambda"), lb[0], lb[1]], axis=0).transpose(2, 0, 1)
    w["lru_w"] = np.stack([i["lru_wa"][0], i["lru_wx"][0]], axis=2)
    w["norm_cols"] = np.stack([i["ln_in_g"].reshape(P, KB), i["ln_in_b"].reshape(P, KB)], axis=1)
    w["norm_rows"] = np.stack([i["ln_in_g"], i["ln_in_b"], i["ln1_g"][0], i["ln1_b"][0], i["ln2_g"][0], i["ln2_b"][0]])
    w["ident"] = np.eye(P, dtype=np.float32)
    s, t = np.arange(P)[:, None] % CHUNK, np.arange(CHUNK)[None]
    w["cmask"] = (s <= t).astype(np.float32)
    r = np.ones((P, TA), np.float32)
    r[:, 0] = 0
    r[:, META::CHUNK] = 0
    w["reset"] = r
    w["router_w"] = i["router_w"][0].reshape(P, KB, E)
    w["router_bias"] = i["router_bias"]
    w["ws_gate_up"] = np.concatenate([i["ws_gate"][0], i["ws_up"][0]], axis=1).reshape(P, KB, 2 * F)
    w["ws_down"] = i["ws_down"][0].reshape(2, P, D).transpose(1, 0, 2)
    w["w_gate_up"] = np.concatenate([i["we_gate"][0], i["we_up"][0]], axis=2).reshape(E, P, 2, CHUNK_W)
    w["w_down"] = i["we_down"][0].reshape(E, 2, P, D).transpose(0, 2, 1, 3).reshape(E, P, CHUNK_W)
    n = np.arange(P)
    w["before"] = (n[:, None] < n[None]).astype(np.float32)
    w["before2"] = w["before"] * (n[:, None] // E == n[None] // E).astype(np.float32)
    w["onehot"] = np.concatenate([np.tile(np.eye(E, dtype=np.float32), (2, 1)), np.zeros((P, EXTRA), np.float32)], axis=1)
    w["two"] = np.tile(np.eye(SLOTS, dtype=np.float32), (2, 1))
    w["iota"] = np.broadcast_to(np.arange(SLOTS, dtype=np.float32), (P, SLOTS))
    w["e_col"] = (n % E).astype(np.float32).reshape(P, 1)
    w["steps64"] = np.broadcast_to(np.arange(1, 13, dtype=np.float32) * SLOTS, (P, 12))
    w["steps4"] = np.broadcast_to(np.arange(12, dtype=np.float32) * QUAD, (P, 12))
    return {k: np.ascontiguousarray(v) for k, v in w.items()}


def kernel(**inputs):
    import concourse.bacc as bacc
    from concourse.bass_utils import run_bass_kernel_spmd

    arrays = {f"in_{n}": v for n, v in layout({n: np.asarray(v) for n, v in inputs.items()}).items()}
    nc = bacc.Bacc("TRN2", target_bir_lowering=False, num_devices=1)
    aps = {n[3:]: nc.dram_tensor(n, v.shape, mybir.dt.from_np(v.dtype), kind="ExternalInput").ap()
           for n, v in arrays.items()}
    out = nc.dram_tensor("out", (T, D), F32, kind="ExternalOutput").ap()
    program(nc, aps, out)
    result = run_bass_kernel_spmd(nc, [arrays], core_ids=[0])
    return result.results[0]["out"].reshape(1, T, D)
```
